# Optimizing a Trainium2 kernel written in Bass

```python
import math
import jax, jax.numpy as jnp
from jax import lax
import numpy as np

D_MODEL = 1024
BATCH = 1
SEQ = 256
DEPTH = 1

D_RNN = 1024
RNN_BLOCKS = 16
RNN_BW = D_RNN // RNN_BLOCKS
CONV_W = 4
LRU_C = 8.0
N_HEADS = 8
HEAD_DIM = 128
D_ATT = N_HEADS * HEAD_DIM
KV_RANK = 256
IDX_HEADS = 8
IDX_DIM = 64
TOPK_MAX = 256
Q_BLOCK = 128
N_BUCKETS = 32
MAX_DIST = 128
N_EXPERTS = 16
N_GROUPS = 4
EXPERTS_PER_GROUP = N_EXPERTS // N_GROUPS
TOP_K_EXPERTS = 2
D_EXPERT = 512
ALPHA = (2 * DEPTH) ** 0.25
BETA = (8 * DEPTH) ** -0.25
LN_EPS = 1e-5
RMS_EPS = 1e-6
SPLITS = (D_RNN, D_RNN, D_ATT, KV_RANK, IDX_HEADS * IDX_DIM, IDX_DIM, IDX_HEADS, D_MODEL, D_MODEL)
D_IN = sum(SPLITS)
SPLIT_AT = tuple(int(v) for v in np.cumsum(SPLITS)[:-1])

kernel_name = "hybrid_rglru_dsa_groupmoe_deepnorm"

def layer_norm(x, g, b):
    xf = x.astype(jnp.float32)
    mu = jnp.mean(xf, axis=-1, keepdims=True)
    var = jnp.mean(jnp.square(xf - mu), axis=-1, keepdims=True)
    return ((xf - mu) * lax.rsqrt(var + LN_EPS) * g + b).astype(x.dtype)

def rms_norm(x, g):
    xf = x.astype(jnp.float32)
    return (xf * lax.rsqrt(jnp.mean(jnp.square(xf), axis=-1, keepdims=True) + RMS_EPS) * g).astype(x.dtype)

def causal_depthwise_conv(x, w, b):
    S = x.shape[1]
    xp = jnp.pad(x, ((0, 0), (CONV_W - 1, 0), (0, 0)))
    return b + sum(w[k] * xp[:, k:k + S] for k in range(CONV_W))

def rg_lru(x, w_a, b_a, w_x, b_x, lam):
    B, S, _ = x.shape
    xb = x.reshape(B, S, RNN_BLOCKS, RNN_BW)
    r = jax.nn.sigmoid(jnp.einsum('bsgi,gij->bsgj', xb, w_a).reshape(B, S, D_RNN) + b_a)
    i = jax.nn.sigmoid(jnp.einsum('bsgi,gij->bsgj', xb, w_x).reshape(B, S, D_RNN) + b_x)
    log_a = (-LRU_C * r.astype(jnp.float32)) * jax.nn.softplus(-lam.astype(jnp.float32))
    a = jnp.exp(log_a)
    u = jnp.sqrt(-jnp.expm1(2.0 * log_a)) * (i * x).astype(jnp.float32)

    def combine(left, right):
        a_l, b_l = left
        a_r, b_r = right
        return a_l * a_r, a_r * b_l + b_r

    _, h = lax.associative_scan(combine, (a, u), axis=1)
    return h.astype(x.dtype)

def t5_bucket(dist):
    max_exact = N_BUCKETS // 2
    d = jnp.maximum(dist, 0)
    large = max_exact + (jnp.log(jnp.maximum(d, 1).astype(jnp.float32) / max_exact)
                         / math.log(MAX_DIST / max_exact) * (N_BUCKETS - max_exact)).astype(jnp.int32)
    large = jnp.minimum(large, N_BUCKETS - 1)
    return jnp.where(d < max_exact, d, large)

def dsa_attention(q, c_kv, q_idx, k_idx, w_idx, w_uk, w_uv, rel_bias):
    B, S = c_kv.shape[:2]
    n_keep = min(TOPK_MAX, S // 4)
    nb = S // Q_BLOCK
    q_lat = jnp.einsum('bshd,hcd->bshc', q, w_uk) * (HEAD_DIM ** -0.5)
    key_pos = jnp.arange(S, dtype=jnp.int32)

    def blocks(a):
        return jnp.swapaxes(a.reshape(B, nb, Q_BLOCK, *a.shape[2:]), 0, 1)

    def one_block(args):
        blk, ql, qi, wi = args
        t = blk * Q_BLOCK + jnp.arange(Q_BLOCK, dtype=jnp.int32)
        sc = jax.nn.relu(jnp.einsum('bqhd,bsd->bqhs', qi, k_idx))
        sc = jnp.einsum('bqhs,bqh->bqs', sc, wi).astype(jnp.float32)
        causal = key_pos[None, :] <= t[:, None]
        sc = jnp.where(causal[None], sc, -jnp.inf)
        _, idx = lax.top_k(sc, n_keep)
        valid = idx <= t[None, :, None]
        kv = jax.vmap(lambda c, ix: c[ix])(c_kv, idx)
        logits = jnp.einsum('bqhc,bqkc->bhqk', ql, kv).astype(jnp.float32)
        bias = rel_bias[t5_bucket(t[None, :, None] - idx)]
        logits = logits + jnp.moveaxis(bias, -1, 1).astype(jnp.float32)
        logits = jnp.where(valid[:, None], logits, -1e30)
        p = jax.nn.softmax(logits, axis=-1).astype(kv.dtype)
        return jnp.einsum('bhqk,bqkc->bqhc', p, kv)

    o_lat = lax.map(one_block, (jnp.arange(nb, dtype=jnp.int32), blocks(q_lat), blocks(q_idx), blocks(w_idx)))
    o_lat = jnp.swapaxes(o_lat, 0, 1).reshape(B, S, N_HEADS, KV_RANK)
    o = jnp.einsum('bshc,hcd->bshd', o_lat, w_uv)
    return o.reshape(B, S, D_ATT)

def token_mixer(x, w_in, conv_w, conv_b, lru_wa, lru_ba, lru_wx, lru_bx, lru_lambda,
                kv_norm, w_uk, w_uv, proj_rnn, proj_att, w_out, rel_bias):
    B, S, _ = x.shape
    h = x @ w_in
    x_rnn, g_rnn, q, c_kv, q_idx, k_idx, w_idx, gate_rnn, gate_att = jnp.split(h, SPLIT_AT, axis=-1)
    xr = causal_depthwise_conv(x_rnn, conv_w, conv_b)
    y_rnn = rg_lru(xr, lru_wa, lru_ba, lru_wx, lru_bx, lru_lambda) * jax.nn.gelu(g_rnn)
    y_att = dsa_attention(q.reshape(B, S, N_HEADS, HEAD_DIM), rms_norm(c_kv, kv_norm),
                          q_idx.reshape(B, S, IDX_HEADS, IDX_DIM) * (IDX_DIM ** -0.5), k_idx,
                          w_idx * (IDX_HEADS ** -0.5), w_uk, w_uv, rel_bias)
    merged = jax.nn.sigmoid(gate_rnn) * (y_rnn @ proj_rnn) + jax.nn.sigmoid(gate_att) * (y_att @ proj_att)
    return merged @ w_out

def grouped_moe(x, w_router, router_bias, w_gate, w_up, w_down):
    B, S, D = x.shape
    tok = x.reshape(B * S, D)
    aff = jax.nn.sigmoid((tok @ w_router).astype(jnp.float32))
    sel = aff + router_bias.astype(jnp.float32)
    grp = sel.reshape(-1, N_GROUPS, EXPERTS_PER_GROUP)
    grp_score = jnp.sum(lax.top_k(grp, TOP_K_EXPERTS)[0], axis=-1)
    g_best = jnp.argmax(grp_score, axis=-1)
    in_group = (jnp.arange(N_EXPERTS) // EXPERTS_PER_GROUP)[None, :] == g_best[:, None]
    _, e_idx = lax.top_k(jnp.where(in_group, sel, -jnp.inf), TOP_K_EXPERTS)
    g = jnp.take_along_axis(aff, e_idx, axis=-1)
    g = g / jnp.sum(g, axis=-1, keepdims=True)
    combine = jnp.sum(jax.nn.one_hot(e_idx, N_EXPERTS, dtype=jnp.float32) * g[..., None], axis=1)
    out = jnp.zeros_like(tok)
    for e in range(N_EXPERTS):
        he = jax.nn.silu(tok @ w_gate[e]) * (tok @ w_up[e])
        out = out + combine[:, e:e + 1].astype(tok.dtype) * (he @ w_down[e])
    return out.reshape(B, S, D)

def setup_inputs(seed: int = 0) -> dict:
    key = jax.random.key(seed)
    ks = jax.random.split(key, 24)
    f32 = jnp.float32
    L = DEPTH

    def nrm(k, shape, scale):
        return jax.random.normal(k, shape, f32) * scale

    u = jax.random.uniform(ks[9], (L, D_RNN), f32, 0.9, 0.999)
    a0 = u ** (1.0 / LRU_C)
    lru_lambda = jnp.log(a0) - jnp.log1p(-a0)
    return {
        "x": nrm(ks[0], (BATCH, SEQ, D_MODEL), 1.0),
        "w_in": nrm(ks[1], (L, D_MODEL, D_IN), D_MODEL ** -0.5),
        "conv_w": nrm(ks[2], (L, CONV_W, D_RNN), CONV_W ** -0.5),
        "conv_b": nrm(ks[3], (L, D_RNN), 0.01),
        "lru_wa": nrm(ks[4], (L, RNN_BLOCKS, RNN_BW, RNN_BW), RNN_BW ** -0.5),
        "lru_ba": nrm(ks[5], (L, D_RNN), 0.01),
        "lru_wx": nrm(ks[6], (L, RNN_BLOCKS, RNN_BW, RNN_BW), RNN_BW ** -0.5),
        "lru_bx": nrm(ks[7], (L, D_RNN), 0.01),
        "lru_lambda": lru_lambda,
        "kv_norm": 1.0 + nrm(ks[8], (L, KV_RANK), 0.02),
        "w_uk": nrm(ks[10], (L, N_HEADS, KV_RANK, HEAD_DIM), KV_RANK ** -0.5),
        "w_uv": nrm(ks[11], (L, N_HEADS, KV_RANK, HEAD_DIM), KV_RANK ** -0.5),
        "proj_rnn": nrm(ks[12], (L, D_RNN, D_MODEL), D_RNN ** -0.5),
        "proj_att": nrm(ks[13], (L, D_ATT, D_MODEL), D_ATT ** -0.5),
        "w_out": nrm(ks[14], (L, D_MODEL, D_MODEL), BETA * D_MODEL ** -0.5),
        "ln1_g": 1.0 + nrm(ks[15], (L, D_MODEL), 0.02),
        "ln1_b": nrm(ks[16], (L, D_MODEL), 0.01),
        "w_router": nrm(ks[17], (D_MODEL, N_EXPERTS), D_MODEL ** -0.5),
        "router_bias": nrm(ks[18], (N_EXPERTS,), 0.01),
        "exp_w_gate": nrm(ks[19], (L, N_EXPERTS, D_MODEL, D_EXPERT), D_MODEL ** -0.5),
        "exp_w_up": nrm(ks[20], (L, N_EXPERTS, D_MODEL, D_EXPERT), D_MODEL ** -0.5),
        "exp_w_down": nrm(ks[21], (L, N_EXPERTS, D_EXPERT, D_MODEL), BETA * D_EXPERT ** -0.5),
        "ln2_g": 1.0 + nrm(ks[22], (L, D_MODEL), 0.02),
        "ln2_b": nrm(ks[23], (L, D_MODEL), 0.01),
        "rel_bias": nrm(jax.random.fold_in(key, 99), (N_BUCKETS, N_HEADS), 0.1),
    }

def reference(x, w_in, conv_w, conv_b, lru_wa, lru_ba, lru_wx, lru_bx, lru_lambda, kv_norm,
              w_uk, w_uv, proj_rnn, proj_att, w_out, ln1_g, ln1_b, w_router, router_bias,
              exp_w_gate, exp_w_up, exp_w_down, ln2_g, ln2_b, rel_bias):
    for l in range(DEPTH):
        mix = token_mixer(x, w_in[l], conv_w[l], conv_b[l], lru_wa[l], lru_ba[l], lru_wx[l], lru_bx[l],
                          lru_lambda[l], kv_norm[l], w_uk[l], w_uv[l], proj_rnn[l], proj_att[l], w_out[l],
                          rel_bias)
        x = layer_norm(ALPHA * x + mix, ln1_g[l], ln1_b[l])
        ffn = grouped_moe(x, w_router, router_bias, exp_w_gate[l], exp_w_up[l], exp_w_down[l])
        x = layer_norm(ALPHA * x + ffn, ln2_g[l], ln2_b[l])
    return x


_drawn_inputs = setup_inputs


def setup_inputs(seed=0):
    import zlib

    import numpy as np

    out = dict(_drawn_inputs(seed))
    spreads = {}
    factors = {'conv_b': 11.475,
     'lru_ba': 192.604,
     'lru_bx': 64.0,
     'kv_norm': 8.0,
     'ln2_g': 22.71,
     'ln2_b': 46.606,
     'rel_bias': 4.384,
     'ln1_b': 3.211}
    for name, (base, spread) in spreads.items():
        noise = np.random.default_rng([zlib.crc32(name.encode()), seed]).standard_normal(out[name].shape)
        drawn = base * np.exp(spread * noise) if base else spread * noise
        out[name] = __import__('jax').numpy.asarray(drawn.astype(out[name].dtype))
    for name, factor in factors.items():
        out[name] = (out[name] * factor).astype(out[name].dtype)
    return out
```

```python
from contextlib import ExitStack

import numpy as np

import concourse.bass as bass
from concourse import mybir

F32 = mybir.dt.float32
I32 = mybir.dt.int32
U32 = mybir.dt.uint32
ALU = mybir.AluOpType
ACT = mybir.ActivationFunctionType
AX = mybir.AxisListType

P = 128
D = 1024
S = 256
KC = D // P
TT = S // P
HEADS = 8
HD = 128
RANK = 256
CC = RANK // P
IDX_HEADS = 8
IDX_DIM = 64
KEEP = 64
CONV = 4
LRU_C = 8.0
BUCKETS = 32
MAX_DIST = 128
EXPERTS = 16
GROUPS = 4
PER_GROUP = EXPERTS // GROUPS
FF = 512
FC = FF // P
ALPHA = 2.0 ** 0.25
LN_EPS = 1e-5
RMS_EPS = 1e-6
SLOTS = 64
PAIRS = EXPERTS // 2
ROUNDS = S // SLOTS
FILL = -3.0e38
TAKEN = -3.4e38
RING = 8
BANKS = 4


def mixer_pieces():
    out = [("ckv", 0), ("ckv", 1), ("kidx", 0)] + [("qidx", c) for c in range(4)]
    out += [("xr", c) for c in range(KC)] + [("g", c) for c in range(KC)]
    out += [("gr", c) for c in range(KC)] + [("ga", c) for c in range(KC)]
    out += [("uk", 0), ("uk", 1), ("uv", 0), ("uv", 1), ("q", 0), ("q", 1)]
    for h in range(HEADS):
        if h + 2 < HEADS:
            out.append(("q", h + 2))
        out.append(("pr", h))
    out += [("pa", c) for c in range(KC)] + [("wo", c) for c in range(KC)]
    return out


PIECES = mixer_pieces()
PIECE_AT = {key: i for i, key in enumerate(PIECES)}
LOADS = [(i, min(2, len(PIECES) - i)) for i in range(0, len(PIECES), 2)]


def mixer_jobs():
    out = [("ckv", 0), ("ckv", 1), ("kidx", 0)] + [("qidx", c) for c in range(4)]
    out += [(k, c) for k in ("xr", "g", "lru", "gr", "ga", "k") for c in range(KC)]
    out += [("v", i) for i in range(4)] + [("q", 0), ("q", 1)]
    for h in range(HEADS):
        if h + 2 < HEADS:
            out.append(("q", h + 2))
        out.append(("pr", h))
    return out + [("pa", c) for c in range(KC)]


JOBS = mixer_jobs()
JOB_AT = {key: j for j, key in enumerate(JOBS)}
SCORE_HEADS = [(0, 2, 4, 6), (1, 3, 5, 7), (0, 2), (1, 3), (4, 6), (5, 7)]
EARLY = (8, 11, 14, 17)
BY_DVE = {"ckv", "q", "v", "pr", "pa"}


def emptied_count(j):
    mine = JOBS[j][0] in BY_DVE
    return mine, sum((k in BY_DVE) == mine for k, _ in JOBS[:j + 1])


def jobs_to_free(i):
    kind, c = PIECES[i]
    last = {"ckv": ("ckv", 1), "uk": ("k", 4 * c + 3), "uv": ("v", 3)}.get(kind, (kind, c))
    return JOB_AT[last] + 1


def hybrid_layer(nc, x, xT, wp, w_widx, conv_w, conv_b, lru_w, lru_ba, lru_bx, lam, kvn, ln1_g, ln1_b,
                 w_router, router_bias, w_gate, w_up, w_down, ln2_g, ln2_b, rel_bias, bucket_hot, out):
    with ExitStack() as ctx:
        def sb(name, shape, dt=F32):
            return ctx.enter_context(nc.sbuf_tensor(name, shape, dt))

        def sem(name):
            return ctx.enter_context(nc.semaphore(name))

        scratch = nc.dram_tensor("bias_scratch", [HEADS, 3 * P], F32, kind="Internal").ap()

        NPAGE = 10
        pages = sb("pages", [P, NPAGE * 2048])
        A_, B_, I_, AP_, T_, XT_, S1_, S2_, R_, F_ = range(NPAGE)

        def page(i, n=1):
            return pages[:, i * 2048:(i + n) * 2048]

        def split(ap, **k):
            names = list(k)
            if len(names) == 1:
                return ap.rearrange("p (a b) -> p a b", a=k[names[0]])
            return ap.rearrange("p (a b c) -> p a b c", a=k[names[0]], b=k[names[1]])

        xrnn = sb("xrnn", [P, KC, S + CONV - 1])
        q_sb = split(page(A_), a=HEADS)
        x1 = split(page(A_), a=TT)
        conv = split(page(B_), a=KC)
        kT = split(page(B_), a=HEADS)
        acc = split(page(B_), a=TT)
        rr = split(page(R_), a=KC)
        merged = split(page(R_), a=KC)
        ii = split(page(I_), a=KC)
        v_sb = split(page(I_), a=TT)
        x1T = split(page(I_), a=KC)
        aa = split(page(AP_), a=KC)
        oT = split(page(AP_), a=HEADS)
        lruw = split(page(T_), a=KC, b=2)
        toep = split(page(T_), a=HEADS)
        lnv = split(page(T_), a=2)
        xT_sb = split(page(XT_), a=KC)
        x_sb = split(page(XT_), a=TT)
        sig_r = split(page(S1_), a=KC)
        sig_a = split(page(S2_), a=KC)
        qiT = split(pages[:, S1_ * 2048:S1_ * 2048 + 1024], a=4)
        kiT = pages[:, S1_ * 2048 + 1024:S1_ * 2048 + 1280]
        relu = split(pages[:, S2_ * 2048:S2_ * 2048 + 1024], a=2)
        gel = split(page(F_), a=KC)
        ring = sb("ring", [P, RING, 1024])
        moe_buf = ring[:, :, :].rearrange("p a b -> p (a b)")
        xg = split(moe_buf[:, 0:2048], a=2, b=KC)
        silu = moe_buf[0:SLOTS, 2048:2560]
        he = moe_buf[0:SLOTS, 2560:3072]
        heT = split(moe_buf[:, 3072:3328], a=FC)
        ysb = moe_buf[:, 3328:4352]
        hot = split(moe_buf[:, 4352:4608], a=TT)
        hotc = split(moe_buf[:, 4608:4864], a=TT)
        spread = split(moe_buf[:, 4864:5120], a=TT)
        ln2v = split(moe_buf[:, 5120:7168], a=2)
        eg0 = sb("eg0", [P, KC, FF])
        eu0 = sb("eu0", [P, KC, FF])
        ed0 = sb("ed0", [P, FC, D])
        eg1 = sb("eg1", [P, KC, FF])
        eu1 = page(S1_, 2).rearrange("p (a b) -> p a b", a=KC)
        ed1 = page(R_, 2).rearrange("p (a b) -> p a b", a=FC)
        ew = [(eg0[:, :, :], eu0[:, :, :], ed0[:, :, :]), (eg1[:, :, :], eu1, ed1)]
        conv_tmp = page(A_)

        xrnn_flat = xrnn[:, :, :].rearrange("p a b -> p (a b)")[:, 0:2048]
        toep_rev = split(xrnn_flat, a=HEADS)
        flip = sb("flip", [P, P])
        ident = sb("ident", [P, P])
        ones = sb("ones", [P, P])
        before = sb("before", [P, P])
        causal = sb("causal", [P, S])
        slot_no = sb("slot_no", [P, (ROUNDS + 1) * SLOTS])
        widx_w = sb("widx_w", [P, KC, IDX_HEADS])
        router_w = sb("router_w", [P, KC, EXPERTS])
        vec = sb("vec", [P, 9 * KC])
        cw = vec[:, 0:4 * KC].rearrange("p (a b) -> p a b", a=CONV)
        cb = vec[:, 4 * KC:5 * KC]
        ba = vec[:, 5 * KC:6 * KC]
        bx = vec[:, 6 * KC:7 * KC]
        lam_sb = vec[:, 7 * KC:8 * KC]
        kvn_sb = vec[:, 8 * KC:8 * KC + CC]
        sp = sb("sp", [P, 8, KC])
        rb_sb = sb("rb_sb", [P, EXPERTS])
        relb = sb("relb", [BUCKETS, HEADS])
        bvec = sb("bvec", [HEADS, 3 * P])
        ckv = sb("ckv", [P, TT, RANK])
        ckvT = sb("ckvT", [P, CC, S])
        wid = sb("wid", [P, TT, IDX_HEADS])
        stat = sb("stat", [P, 16])
        sc = sb("sc", [P, 3 * P])
        work = sb("work", [P, 3 * P])
        top = sb("top", [P, 8])
        bm = sb("bm", [P, 2, 3 * P])
        lg = sb("lg", [P, 2, 3 * P])
        pT = sb("pT", [P, 3 * P])
        bhot = pT[0:BUCKETS, :]
        hst = sb("hst", [P, 2, 8])
        stats = sb("stats", [P, TT, 2, 6])
        mv = sb("mv", [P, TT, 4])
        rt = sb("rt", [P, TT, 96])
        cnt = sb("cnt", [P, 4])
        cnt_i = sb("cnt_i", [P, 4], I32)
        tmpm = lg[:, 0, 0:S]

        ps = [ctx.enter_context(nc.psum_tensor(f"ps{i}", [P, 512], F32)) for i in range(8)]

        s_small = sem("small_loaded")
        s_xT = sem("xT_loaded")
        s_lruw = sem("lruw_loaded")
        s_lruz = sem("lruw_zeroed")
        s_ring = [sem(f"ring_loaded{i}") for i in range(RING // 2)]
        s_x = sem("x_loaded")
        s_bvec = sem("bias_vector")
        s_bput = sem("bias_stored")
        s_toep = sem("toeplitz_loaded")
        s_tfp = sem("toeplitz_in_psum")
        s_tf = sem("toeplitz_ready")
        s_ln1 = sem("ln1_vectors")
        s_ln2 = sem("ln2_vectors")
        s_const = sem("constants")
        s_job = sem("job_done")
        s_actE = sem("emptied_by_act")
        s_dveE = sem("emptied_by_dve")
        s_sq = sem("ckv_squares")
        s_ms = sem("ckv_mean_squares")
        s_rms = sem("ckv_root")
        s_ckv = sem("ckv_ready")
        s_ckvTp = sem("ckvT_in_psum")
        s_ckvT = sem("ckvT_ready")
        s_scp = sem("scores_in_psum")
        s_relu = sem("relu_done")
        s_racc = sem("relu_used")
        s_bvp = sem("bias_in_psum")
        s_spe = sem("exp_lambda")
        s_sp = sem("softplus_ready")
        s_conv = sem("conv_ready")
        s_at = sem("decay_ready")
        s_sqa = sem("sqrt_arg")
        s_sqo = sem("sqrt_done")
        s_y = sem("y_rnn_ready")
        s_bm = sem("bias_mask_ready")
        s_bmu = sem("bias_mask_used")
        s_mask = sem("mask_ready")
        s_lp = sem("logits_in_psum")
        s_lm = sem("logits_max")
        s_exp = sem("exp_done")
        s_pn = sem("probs_ready")
        s_ptp = sem("probsT_in_psum")
        s_pt = sem("probsT_ready")
        s_op = sem("o_in_psum")
        s_o = sem("o_ready")
        s_wo = sem("mix_in_psum")
        s_var = sem("variance")
        s_std = sem("deviation")
        s_x1 = sem("x1_ready")
        s_x1Tp = sem("x1T_in_psum")
        s_x1T = sem("x1T_ready")
        s_rl = sem("router_in_psum")
        s_aff = sem("affinity")
        s_msk = sem("choice_ready")
        s_pos = sem("positions_in_psum")
        s_cnt = sem("count_ready")
        s_hot = sem("one_hot_ready")
        s_hotc = sem("gate_hot_ready")
        s_xgp = sem("gathered_in_psum")
        s_xg = sem("gathered_ready")
        s_wl = [[sem(f"w{'gud'[u]}{e}_loaded") for u in range(3)] for e in range(2)]
        s_hp = sem("hidden_in_psum")
        s_si = sem("silu_done")
        s_he = sem("hidden_ready")
        s_turn = sem("hidden_may_be_transposed")
        s_htp = sem("hiddenT_in_psum")
        s_ht = sem("hiddenT_ready")
        s_yp = sem("y_in_psum")
        s_ys = sem("y_ready")
        s_gp = sem("spread_in_psum")
        s_g = sem("spread_ready")
        s_sp4 = sem("spread_out_in_psum")
        s_ac = sem("accumulated")
        s_fin = sem("result_ready")
        s_out = sem("result_stored")
        s_v = sem("vector_chain")
        s_a = sem("scalar_chain")
        s_p = sem("pool_chain")

        SMALL = 14
        block = ctx.enter_context(nc.Block())

        def piece(i):
            return ring[:, i % RING, :]

        def expert_ap(u, p, e):
            src = (w_gate, w_up, w_down)[u]
            a = KC if u < 2 else FC
            return src[bass.ds(p * 2 + e, 1), :, :].rearrange("o p (a b) -> (o p) a b", a=a)

        @block.sync
        def _(sp_e):
            sp_e.dma_start(xT_sb, xT).then_inc(s_xT, 16)

            def ring_load(n):
                i, m = LOADS[n]
                if i >= RING:
                    sp_e.wait_ge(s_job, jobs_to_free(i + m - 1 - RING))
                sp_e.dma_start(ring[:, i % RING:i % RING + m, :],
                               wp[i:i + m, :, :].rearrange("a p b -> p a b")).then_inc(s_ring[n % 4], 16)

            ring_load(0)
            for dst, src in ((widx_w[:, :, :], w_widx), (cw, conv_w), (cb, conv_b), (ba, lru_ba), (bx, lru_bx),
                             (lam_sb, lam), (kvn_sb, kvn), (router_w[:, :, :], w_router), (relb[:, :], rel_bias),
                             (bhot, bucket_hot), (rb_sb[:, :], router_bias.partition_broadcast(P))):
                sp_e.dma_start(dst, src).then_inc(s_small, 16)
            for n in (1, 2, 3):
                ring_load(n)
            sp_e.wait_ge(s_lruz, 1)
            for par in range(2):
                for m in range(2):
                    sp_e.dma_start(lruw[64 * par:64 * par + 64, :, m, 64 * par:64 * par + 64],
                                   lru_w[par, m].rearrange("i c j -> i c j")).then_inc(s_lruw, 16)
            for n in range(4, len(LOADS)):
                ring_load(n)
                if n == 6:
                    sp_e.wait_ge(s_bvec, 1)
                    sp_e.dma_start(scratch, bvec[:, :]).then_inc(s_bput, 16)
                if n in EARLY:
                    e, u = divmod(EARLY.index(n), 3)
                    sp_e.dma_start(ew[e][u], expert_ap(u, 0, e)).then_inc(s_wl[e][u], 16)
                if LOADS[n][0] <= PIECE_AT[("gr", 2)] < LOADS[n][0] + 2:
                    sp_e.wait_ge(s_conv, KC)
                    sp_e.wait_ge(s_bput, 16)
                    sp_e.dma_start(toep_rev, bass.AP(tensor=scratch.tensor, offset=scratch.offset,
                                                     ap=[[1, P], [3 * P, HEADS], [1, S]])).then_inc(s_toep, 16)
                if LOADS[n][0] <= PIECE_AT[("wo", 0)] < LOADS[n][0] + 2:
                    sp_e.wait_ge(s_job, JOB_AT[("q", HEADS - 1)] + 1)
                    sp_e.dma_start(x_sb, x.rearrange("(t p) d -> p t d", p=P)).then_inc(s_x, 16)
                    sp_e.wait_ge(s_bm, HEADS)
                    sp_e.dma_start(lnv[:, 0, :], ln1_g.partition_broadcast(P)).then_inc(s_ln1, 16)
                    sp_e.dma_start(lnv[:, 1, :], ln1_b.partition_broadcast(P)).then_inc(s_ln1, 16)
            sp_e.wait_ge(s_dveE, emptied_count(JOB_AT[("pa", KC - 1)])[1])
            sp_e.dma_start(eu1, expert_ap(1, 0, 1)).then_inc(s_wl[1][1], 16)
            sp_e.wait_ge(s_wo, 2)
            sp_e.dma_start(ed1, expert_ap(2, 0, 1)).then_inc(s_wl[1][2], 16)
            sp_e.dma_start(ln2v[:, 0, :], ln2_g.partition_broadcast(P)).then_inc(s_ln2, 16)
            sp_e.dma_start(ln2v[:, 1, :], ln2_b.partition_broadcast(P)).then_inc(s_ln2, 16)

            def load_pair(n, p):
                for e in range(2):
                    for u in range(3):
                        if u < 2:
                            sp_e.wait_ge(s_hp, n * 4 + (2 * e + u + 1))
                        else:
                            sp_e.wait_ge(s_yp, n * 2 + (e + 1))
                        sp_e.dma_start(ew[e][u], expert_ap(u, p, e)).then_inc(s_wl[e][u], 16)

            with sp_e.Fori(0, PAIRS - 1) as p:
                load_pair(p, p + 1)
            sp_e.wait_ge(s_cnt, 1)
            for b in range(1, ROUNDS):
                with sp_e.If(sp_e.value_load(cnt_i[0:1, b:b + 1], min_val=0, max_val=1)):
                    with sp_e.Fori(0, PAIRS) as p:
                        load_pair(p + (PAIRS * b - 1), p)
            sp_e.wait_ge(s_fin, 1)
            sp_e.dma_start(out[0:P, :], acc[:, 0, :]).then_inc(s_out, 16)
            sp_e.wait_ge(s_fin, 2)
            sp_e.dma_start(out[P:S, :], acc[:, 1, :]).then_inc(s_out, 16)
            sp_e.wait_ge(s_out, 32)

        @block.gpsimd
        def _(pool):
            pool.memset(page(T_), 0.0).then_inc(s_lruz, 1)
            pool.memset(ident[:, :], 0.0).then_inc(s_p, 1)
            pool.memset(flip[:, :], 0.0).then_inc(s_p, 1)
            pool.memset(before[:, :], 1.0).then_inc(s_p, 1)
            pool.memset(causal[:, :], 0.0).then_inc(s_p, 1)
            pool.memset(ones[:, :], 1.0).then_inc(s_const, 1)
            pool.wait_ge(s_p, 4)
            pool.affine_select(out=flip[:, :], in_=flip[:, :], compare_op=ALU.not_equal, fill=1.0, base=1 - P,
                               pattern=[[1, P]], channel_multiplier=1).then_inc(s_const, 1)
            pool.affine_select(out=ident[:, :], in_=ident[:, :], compare_op=ALU.not_equal, fill=1.0, base=0,
                               pattern=[[-1, P]], channel_multiplier=1).then_inc(s_const, 1)
            pool.affine_select(out=before[:, :], in_=before[:, :], compare_op=ALU.is_gt, fill=0.0, base=0,
                               pattern=[[1, P]], channel_multiplier=-1).then_inc(s_const, 1)
            pool.affine_select(out=causal[:, :], in_=causal[:, :], compare_op=ALU.is_ge, fill=FILL, base=P,
                               pattern=[[-1, S]], channel_multiplier=1).then_inc(s_const, 1)
            pool.iota(slot_no[:, :], pattern=[[1, (ROUNDS + 1) * SLOTS]], base=0, channel_multiplier=0,
                      allow_small_or_imprecise_dtypes=True).then_inc(s_const, 1)
            pool.wait_ge(s_mask, 1)
            pool.wait_ge(s_tf, 4)
            for h in range(HEADS):
                if h >= 2:
                    pool.wait_ge(s_bmu, h - 1)
                pool.tensor_tensor(bm[:, h % 2, 0:P], toep[:, h, P:S], work[:, 0:P], ALU.add)
                pool.tensor_tensor(bm[:, h % 2, P:3 * P], toep[:, h, :], work[:, P:3 * P], ALU.add).then_inc(s_bm, 1)

        @block.scalar
        def _(act):
            chain = [0]

            def link(ins):
                chain[0] += 1
                ins.then_inc(s_a, 1)
                act.wait_ge(s_a, chain[0])

            for free in (s_si, s_ht, s_ys):
                act.sem_inc(free, 1)
            act.wait_ge(s_small, 11 * 16)
            link(act.activation(sp[:, 0, :], lam_sb, ACT.Abs))
            act.activation(sp[:, 1, :], sp[:, 0, :], ACT.Exp, scale=-1.0).then_inc(s_spe, 1)

            def job(kind, c):
                j = JOB_AT[(kind, c)]
                act.wait_ge(s_job, j + 1)
                return ps[j % BANKS]

            for t in range(TT):
                b = job("ckv", t)
                act.activation(lg[:, t, 0:RANK], b[:, 0:RANK], ACT.Square, accum_out=stat[:, t:t + 1]).then_inc(s_sq, 1)
            act.wait_ge(s_ms, 2)
            act.activation(stat[:, 4:6], stat[:, 2:4], ACT.Sqrt).then_inc(s_rms, 1)
            act.activation(kiT, job("kidx", 0)[:, 0:S], ACT.Copy).then_inc(s_actE, 1)
            for c in range(4):
                act.activation(qiT[:, c, :], job("qidx", c)[:, 0:S], ACT.Copy).then_inc(s_actE, 1)
            act.wait_ge(s_bvp, 1)
            act.activation(bvec[:, :], ps[6][0:HEADS, 0:3 * P], ACT.Copy).then_inc(s_bvec, 1)

            def x_rnn(c):
                b = job("xr", c)
                act.activation(xrnn[:, c, CONV - 1:], b[:, 0:S], ACT.Copy).then_inc(s_a, 1)
                chain[0] += 1
                act.activation(conv[:, c, :], b[:, 0:S], ACT.Identity, bias=cb[:, c:c + 1],
                               scale=cw[:, CONV - 1, c:c + 1]).then_inc(s_actE, 1)

            for g in range(6):
                act.wait_ge(s_scp, g + 1)
                if g >= 2:
                    act.wait_ge(s_racc, g - 1)
                act.activation(relu[:, g % 2, :], ps[4 + g % 2][:, :], ACT.Relu, scale=IDX_DIM ** -0.5).then_inc(s_relu, 1)
                x_rnn(g)
            x_rnn(6)
            x_rnn(7)
            for c in range(KC):
                act.activation(gel[:, c, :], job("g", c)[:, 0:S], ACT.Gelu_apprx_tanh).then_inc(s_actE, 1)
            for c in range(KC):
                b = job("lru", c)
                act.activation(rr[:, c, :], b[:, 0:S], ACT.Sigmoid, bias=ba[:, c:c + 1]).then_inc(s_a, 1)
                chain[0] += 1
                act.activation(ii[:, c, :], b[:, S:2 * S], ACT.Sigmoid, bias=bx[:, c:c + 1]).then_inc(s_actE, 1)
            act.wait_ge(s_racc, 6)
            for c in range(3):
                act.activation(sig_r[:, c, :], job("gr", c)[:, 0:S], ACT.Sigmoid).then_inc(s_actE, 1)
            act.wait_ge(s_sp, 1)
            act.wait_ge(s_a, chain[0])
            for c in range(KC):
                act.activation(aa[:, c, :], rr[:, c, :], ACT.Exp, scale=sp[:, 7, c:c + 1]).then_inc(s_a, 1)
                chain[0] += 1
            act.wait_ge(s_a, chain[0])
            for c in range(KC):
                act.activation(rr[:, c, :], rr[:, c, :], ACT.Tanh, scale=sp[:, 6, c:c + 1]).then_inc(s_at, 1)
            for c in range(3, KC):
                act.activation(sig_r[:, c, :], job("gr", c)[:, 0:S], ACT.Sigmoid).then_inc(s_actE, 1)
            for i in range(4):
                act.wait_ge(s_tfp, i + 1)
                act.activation(page(T_)[:, i * 512:(i + 1) * 512], ps[4 + i][:, :], ACT.Copy).then_inc(s_tf, 1)
            for c in range(4):
                act.activation(sig_a[:, c, :], job("ga", c)[:, 0:S], ACT.Sigmoid).then_inc(s_actE, 1)
            act.wait_ge(s_sqa, 1)
            act.activation(page(R_), page(R_), ACT.Sqrt, scale=2.0).then_inc(s_sqo, 1)
            for c in range(4, KC):
                act.activation(sig_a[:, c, :], job("ga", c)[:, 0:S], ACT.Sigmoid).then_inc(s_actE, 1)
            act.wait_ge(s_conv, KC + 1)
            for h in range(HEADS):
                act.activation(kT[:, h, :], job("k", h)[:, 0:S], ACT.Copy).then_inc(s_actE, 1)
            for h in range(HEADS + 1):
                if h < HEADS:
                    act.wait_ge(s_lm, h + 1)
                    b = h % 2
                    act.activation(lg[:, b, 0:P], lg[:, b, 0:P], ACT.Exp, bias=hst[:, b, 2:3],
                                   accum_out=hst[:, b, 4:5]).then_inc(s_exp, 1)
                    act.activation(lg[:, b, P:3 * P], lg[:, b, P:3 * P], ACT.Exp, bias=hst[:, b, 3:4],
                                   accum_out=hst[:, b, 5:6]).then_inc(s_exp, 1)
                if h >= 1:
                    act.wait_ge(s_ptp, h)
                    act.activation(pT[:, :], ps[6][:, 0:3 * P], ACT.Copy).then_inc(s_pt, 1)
                    act.wait_ge(s_op, h)
                    if h == 1:
                        act.wait_ge(s_y, 1)
                    act.activation(oT[:, h - 1, :], ps[7][:, 0:S], ACT.Copy).then_inc(s_o, 1)
            for t in range(TT):
                act.wait_ge(s_var, t + 1)
                act.activation(mv[:, t, 2:3], mv[:, t, 2:3], ACT.Sqrt).then_inc(s_std, 1)
                for k in range(2):
                    act.wait_ge(s_x1Tp, 2 * t + k + 1)
                    act.activation(x1T[:, 4 * k:4 * k + 4, t * P:(t + 1) * P], ps[4 + k][:, :].rearrange("p (a b) -> p a b", a=4),
                                   ACT.Copy).then_inc(s_x1T, 1)
                act.wait_ge(s_rl, t + 1)
                act.activation(rt[:, t, 0:EXPERTS], ps[6 + t][:, 0:EXPERTS], ACT.Sigmoid).then_inc(s_aff, 1)

            def gathered(count, k, dst):
                act.wait_ge(s_xgp, count)
                act.activation(dst[:, 4 * k:4 * k + 4, :], ps[3 + k][:, :].rearrange("p (a b) -> p a b", a=4),
                               ACT.Copy).then_inc(s_xg, 1)

            def pair(n, par):
                for e in range(2):
                    act.wait_ge(s_hp, n * 4 + (2 * e + 1))
                    act.wait_ge(s_he, n * 2 + (e + 1))
                    act.activation(silu, ps[0][0:SLOTS, :], ACT.Silu).then_inc(s_si, 1)
                    if e == 0:
                        gathered(n * 2 + 3, 0, xg[:, 1 - par])
                    act.wait_ge(s_htp, n * 2 + (e + 2))
                    act.activation(heT, ps[2][:, 0:FC * SLOTS].rearrange("p (a b) -> p a b", a=FC), ACT.Copy).then_inc(s_ht, 1)
                    if e == 0:
                        gathered(n * 2 + 4, 1, xg[:, 1 - par])
                    act.wait_ge(s_yp, n * 2 + (e + 1))
                    act.wait_ge(s_sp4, n * 4 + 1)
                    for f in range(2):
                        act.activation(ysb[64 * e:64 * e + 64, f * 512:(f + 1) * 512], ps[5 + f][64 * e:64 * e + 64, :],
                                       ACT.Copy).then_inc(s_ys, 1)

            gathered(1, 0, xg[:, 0])
            gathered(2, 1, xg[:, 0])
            with act.Fori(0, PAIRS, 2) as p:
                pair(p, 0)
                pair(p + 1, 1)
            for b in range(1, ROUNDS):
                with act.If(act.value_load(cnt_i[0:1, b:b + 1], min_val=0, max_val=1)):
                    with act.Fori(0, PAIRS, 2) as p:
                        pair(p + PAIRS * b, 0)
                        pair(p + (PAIRS * b + 1), 1)
            for t in range(TT):
                act.wait_ge(s_var, TT + t + 1)
                act.activation(mv[:, t, 2:3], mv[:, t, 2:3], ACT.Sqrt).then_inc(s_std, 1)

        @block.tensor
        def _(pe):
            def need(kind, c):
                i = PIECE_AT[(kind, c)]
                n = i // 2
                pe.wait_ge(s_ring[n % 4], 16 * (n // 4 + 1))
                return piece(i)

            def start_job(kind, c):
                j = JOB_AT[(kind, c)]
                if j >= BANKS:
                    by_dve, n = emptied_count(j - BANKS)
                    pe.wait_ge(s_dveE if by_dve else s_actE, n)
                return ps[j % BANKS]

            for free in (s_htp, s_sp4):
                pe.sem_inc(free, 1)
            pe.wait_ge(s_xT, 16)
            for c in range(CC):
                w = need("ckv", c).rearrange("p (k n) -> p k n", k=KC)
                for t in range(TT):
                    for k in range(KC):
                        ins = pe.matmul(ps[t][:, c * P:(c + 1) * P], xT_sb[:, k, t * P:(t + 1) * P], w[:, k, :],
                                        start=(k == 0), stop=(k == KC - 1))
            pe.wait_ge(s_small, 11 * 16)
            for t in range(TT):
                for k in range(KC):
                    ins = pe.matmul(ps[t][:, RANK:RANK + IDX_HEADS], xT_sb[:, k, t * P:(t + 1) * P], widx_w[:, k, :],
                                    start=(k == 0), stop=(k == KC - 1))
                ins.then_inc(s_job, 1)

            def plain(kind, c, rhs, wait=None):
                w = need(kind, c)
                o = start_job(kind, c)
                if wait:
                    pe.wait_ge(*wait)
                for k in range(KC):
                    ins = pe.matmul(o[:, 0:S], w[:, k * P:(k + 1) * P], rhs[:, k, :], start=(k == 0), stop=(k == KC - 1))
                ins.then_inc(s_job, 1)

            plain("kidx", 0, xT_sb)
            for c in range(4):
                plain("qidx", c, xT_sb)
            pe.matmul(ps[6][0:HEADS, 0:3 * P], relb[:, :], bhot, start=True, stop=True).then_inc(s_bvp, 1)

            pe.wait_ge(s_actE, 5)

            def scores(g):
                if g >= 2:
                    pe.wait_ge(s_relu, g - 1)
                t = 0 if g < 2 else 1
                n = P if t == 0 else S
                for i, h in enumerate(SCORE_HEADS[g]):
                    r = 64 * (h % 2)
                    ins = pe.matmul(ps[4 + g % 2][:, i * n:(i + 1) * n], qiT[r:r + 64, h // 2, t * P:(t + 1) * P],
                                    kiT[r:r + 64, 0:n], start=True, stop=True)
                ins.then_inc(s_scp, 1)

            for c in range(KC):
                if c < 6:
                    scores(c)
                plain("xr", c, xT_sb)
            pe.wait_ge(s_const, 6)
            pe.wait_ge(s_ckv, TT)
            for c in range(CC):
                for t in range(TT):
                    ins = pe.transpose(ps[7][:, c * S + t * P:c * S + (t + 1) * P], ckv[:, t, c * P:(c + 1) * P], ident[:, :])
            ins.then_inc(s_ckvTp, 1)
            for c in range(KC):
                plain("g", c, xT_sb)
            pe.wait_ge(s_lruw, 64)
            for c in range(KC):
                o = start_job("lru", c)
                pe.wait_ge(s_conv, c + 1)
                for m in range(2):
                    ins = pe.matmul(o[:, m * S:(m + 1) * S], lruw[:, c, m, :], conv[:, c, :], start=True, stop=True)
                ins.then_inc(s_job, 1)
            for c in range(KC):
                plain("gr", c, xT_sb)
            pe.wait_ge(s_toep, 16)
            pe.wait_ge(s_relu, 6)
            pe.wait_ge(s_bvec, 1)
            pe.wait_ge(s_ckvT, 2)
            for i in range(4):
                pe.matmul(ps[4 + i][:, :], flip[:, :], xrnn_flat[:, i * 512:(i + 1) * 512], start=True,
                          stop=True).then_inc(s_tfp, 1)
            for c in range(KC):
                plain("ga", c, xT_sb)
            pe.wait_ge(s_ckvT, 2)
            for h in range(HEADS):
                w = need("uk", h // 4).rearrange("p (h c d) -> p h c d", h=4, c=CC)
                o = start_job("k", h)
                for c in range(CC):
                    ins = pe.matmul(o[:, 0:S], w[:, h % 4, c, :], ckvT[:, c, :], start=(c == 0), stop=(c == CC - 1))
                ins.then_inc(s_job, 1)
            wv = [need("uv", c) for c in range(CC)]
            for i in range(4):
                t, f = i // 2, i % 2
                o = start_job("v", i)
                for c in range(CC):
                    ins = pe.matmul(o[:, :], ckvT[:, c, t * P:(t + 1) * P], wv[c][:, f * 512:(f + 1) * 512],
                                    start=(c == 0), stop=(c == CC - 1))
                ins.then_inc(s_job, 1)
            plain("q", 0, xT_sb)
            plain("q", 1, xT_sb)

            def logits(h):
                pe.wait_ge(s_dveE, emptied_count(JOB_AT[("q", h)])[1])
                pe.wait_ge(s_actE, emptied_count(JOB_AT[("k", h)])[1])
                if h >= 2:
                    pe.wait_ge(s_lm, h - 1)
                o = ps[4 + h % 2]
                pe.matmul(o[:, 0:P], q_sb[:, h, 0:P], kT[:, h, 0:P], start=True, stop=True)
                pe.matmul(o[:, P:3 * P], q_sb[:, h, P:S], kT[:, h, :], start=True, stop=True).then_inc(s_lp, 1)

            def probs_T(h):
                pe.wait_ge(s_pn, h + 1)
                if h >= 1:
                    pe.wait_ge(s_pt, h)
                for i in range(3):
                    ins = pe.transpose(ps[6][:, i * P:(i + 1) * P], lg[:, h % 2, i * P:(i + 1) * P], ident[:, :])
                ins.then_inc(s_ptp, 1)

            def values(h):
                pe.wait_ge(s_pt, h + 1)
                if h >= 1:
                    pe.wait_ge(s_o, h)
                pe.matmul(ps[7][:, 0:S], v_sb[:, 0, h * HD:(h + 1) * HD], pT[:, 0:S], start=True, stop=False)
                pe.matmul(ps[7][:, P:S], v_sb[:, 1, h * HD:(h + 1) * HD], pT[:, S:3 * P], start=False,
                          stop=True).then_inc(s_op, 1)

            for h in range(HEADS + 1):
                if h < HEADS:
                    logits(h)
                if h + 2 < HEADS:
                    plain("q", h + 2, xT_sb)
                if h >= 1:
                    probs_T(h - 1)
                if h < HEADS:
                    plain("pr", h, gel, (s_y, 1))
                if h >= 1:
                    values(h - 1)
            for c in range(KC):
                plain("pa", c, oT, (s_o, HEADS))

            last = emptied_count(JOB_AT[("pa", KC - 1)])[1]
            pe.wait_ge(s_dveE, last)
            for k in range(0, KC, 1):
                need("wo", k)
            for t in range(TT):
                for f in range(2):
                    for k in range(KC):
                        ins = pe.matmul(ps[2 * t + f][:, :], merged[:, k, t * P:(t + 1) * P],
                                        piece(PIECE_AT[("wo", k)])[:, f * 512:(f + 1) * 512],
                                        start=(k == 0), stop=(k == KC - 1))
                ins.then_inc(s_wo, 1)

            for t in range(TT):
                pe.wait_ge(s_x1, t + 1)
                for k in range(2):
                    if t >= 1:
                        pe.wait_ge(s_x1T, 2 * t - 1 + k)
                    for i in range(4):
                        ins = pe.transpose(ps[4 + k][:, i * P:(i + 1) * P],
                                           x1[:, t, (4 * k + i) * P:(4 * k + i + 1) * P], ident[:, :])
                    ins.then_inc(s_x1Tp, 1)
                pe.wait_ge(s_x1T, 2 * t + 2)
                for k in range(KC):
                    ins = pe.matmul(ps[6 + t][:, 0:EXPERTS], x1T[:, k, t * P:(t + 1) * P], router_w[:, k, :],
                                    start=(k == 0), stop=(k == KC - 1))
                ins.then_inc(s_rl, 1)
            pe.wait_ge(s_msk, TT)
            m0, m1 = rt[:, 0, 32:48], rt[:, 1, 32:48]
            pe.matmul(ps[2][:, 0:16], before[:, :], m0, start=True, stop=True)
            pe.matmul(ps[2][:, 16:32], ones[:, :], m0, start=True, stop=False)
            pe.matmul(ps[2][:, 16:32], before[:, :], m1, start=False, stop=True)
            pe.matmul(ps[2][:, 32:48], ones[:, :], m0, start=True, stop=False)
            pe.matmul(ps[2][:, 32:48], ones[:, :], m1, start=False, stop=True).then_inc(s_pos, 1)

            def gather(k):
                for i in range(4):
                    for t in range(TT):
                        ins = pe.matmul(ps[3 + k][:, i * P:(i + 1) * P],
                                        x1[:, t, (4 * k + i) * P:(4 * k + i + 1) * P], hot[:, t, :],
                                        start=(t == 0), stop=(t == TT - 1))
                ins.then_inc(s_xgp, 1)

            def gather_next(n, k):
                pe.wait_ge(s_hot, n + 2)
                pe.wait_ge(s_xg, n * 2 + (k + 1))
                gather(k)

            def hidden(n, e, par):
                pe.wait_ge(s_xg, n * 2 + 2)
                for u in range(2):
                    pe.wait_ge(s_wl[e][u], n * 16 + 16)
                    if u == 0:
                        pe.wait_ge(s_si, n * 2 + (e + 1))
                    else:
                        pe.wait_ge(s_he, n * 2 + (e + 1))
                    for k in range(KC):
                        ins = pe.matmul(ps[u][0:SLOTS, :], xg[:, par, k, 64 * e:64 * e + 64], ew[e][u][:, k, :],
                                        start=(k == 0), stop=(k == KC - 1))
                    ins.then_inc(s_hp, 1)

            def hidden_T(n, e):
                pe.wait_ge(s_he, n * 2 + (e + 2))
                pe.wait_ge(s_ht, n * 2 + (e + 1))
                pe.sem_inc(s_turn, 1)
                for f in range(FC):
                    ins = pe.transpose(ps[2][:, f * SLOTS:(f + 1) * SLOTS], he[:, f * P:(f + 1) * P],
                                       ident[0:SLOTS, 0:SLOTS])
                ins.then_inc(s_htp, 1)

            def down(n, e):
                pe.wait_ge(s_wl[e][2], n * 16 + 16)
                pe.wait_ge(s_ht, n * 2 + (e + 2))
                pe.wait_ge(s_ys, n * 4 + (2 * e + 1))
                for f in range(2):
                    for k in range(FC):
                        ins = pe.matmul(ps[5 + f][64 * e:64 * e + 64, :], heT[:, k, :],
                                        ew[e][2][:, k, f * 512:(f + 1) * 512], start=(k == 0), stop=(k == FC - 1))
                ins.then_inc(s_yp, 1)

            def spread_T(n):
                pe.wait_ge(s_hotc, n + 1)
                pe.wait_ge(s_ac, n * 4 + 1)
                for t in range(TT):
                    ins = pe.transpose(ps[7][:, t * P:(t + 1) * P], hotc[:, t, :], ident[:, :])
                ins.then_inc(s_gp, 1)

            def spread_out(n):
                pe.wait_ge(s_g, n + 1)
                pe.wait_ge(s_ys, n * 4 + 5)
                for i in range(4):
                    t, f = i // 2, i % 2
                    pe.wait_ge(s_ac, n * 4 + (i + 1))
                    pe.matmul(ps[7][:, :], spread[:, t, :], ysb[:, f * 512:(f + 1) * 512], start=True,
                              stop=True).then_inc(s_sp4, 1)

            def pair(n, par):
                hidden(n, 0, par)
                spread_T(n)
                gather_next(n, 0)
                hidden_T(n, 0)
                gather_next(n, 1)
                down(n, 0)
                hidden(n, 1, par)
                hidden_T(n, 1)
                down(n, 1)
                spread_out(n)

            pe.wait_ge(s_hot, 1)
            gather(0)
            gather(1)
            with pe.Fori(0, PAIRS, 2) as p:
                pair(p, 0)
                pair(p + 1, 1)
            for b in range(1, ROUNDS):
                with pe.If(pe.value_load(cnt_i[0:1, b:b + 1], min_val=0, max_val=1)):
                    with pe.Fori(0, PAIRS, 2) as p:
                        pair(p + PAIRS * b, 0)
                        pair(p + (PAIRS * b + 1), 1)

        @block.vector
        def _(dve):
            chain = [0]

            def link(ins):
                chain[0] += 1
                ins.then_inc(s_v, 1)
                dve.wait_ge(s_v, chain[0])

            def job(kind, c):
                j = JOB_AT[(kind, c)]
                dve.wait_ge(s_job, j + 1)
                return ps[j % BANKS]

            for free in (s_he, s_ac):
                dve.sem_inc(free, 1)
            link(dve.memset(xrnn[:, :, 0:CONV - 1], 0.0))
            dve.wait_ge(s_spe, 1)
            z, w, w2, h_ = sp[:, 1, :], sp[:, 2, :], sp[:, 3, :], sp[:, 4, :]
            link(dve.tensor_scalar(w, z, 2.0, None, ALU.add))
            link(dve.reciprocal(w, w))
            link(dve.tensor_tensor(w, w, z, ALU.mult))
            link(dve.tensor_tensor(w2, w, w, ALU.mult))
            link(dve.tensor_scalar(h_, w2, 1.0 / 17, 1.0 / 15, ALU.mult, ALU.add))
            for d in (13, 11, 9, 7, 5, 3, 1):
                link(dve.tensor_tensor(h_, h_, w2, ALU.mult))
                link(dve.tensor_scalar(h_, h_, 1.0 / d, None, ALU.add))
            link(dve.tensor_tensor(h_, h_, w, ALU.mult))
            link(dve.tensor_scalar(sp[:, 5, :], lam_sb, -1.0, 0.0, ALU.mult, ALU.max))
            link(dve.scalar_tensor_tensor(sp[:, 5, :], h_, 2.0, sp[:, 5, :], ALU.mult, ALU.add))
            link(dve.tensor_scalar(sp[:, 6, :], sp[:, 5, :], LRU_C, None, ALU.mult))
            dve.tensor_scalar(sp[:, 7, :], sp[:, 5, :], -LRU_C, None, ALU.mult).then_inc(s_sp, 1)

            for t in range(TT):
                dve.wait_ge(s_sq, t + 1)
                dve.tensor_scalar(stat[:, 2 + t:3 + t], stat[:, t:t + 1], 1.0 / RANK, RMS_EPS, ALU.mult,
                                  ALU.add).then_inc(s_ms, 1)
            dve.wait_ge(s_rms, 1)
            link(dve.reciprocal(stat[:, 6:8], stat[:, 4:6]))
            for t in range(TT):
                b = job("ckv", t)
                dve.tensor_scalar(ckv[:, t, :], b[:, 0:RANK], stat[:, 6 + t:7 + t], None, ALU.mult).then_inc(s_ckv, 1)
                dve.tensor_scalar(wid[:, t, :], b[:, RANK:RANK + IDX_HEADS], IDX_HEADS ** -0.5, None,
                                  ALU.mult).then_inc(s_dveE, 1)
            dve.wait_ge(s_dveE, 2)
            dve.wait_ge(s_const, 6)
            for g in range(6):
                dve.wait_ge(s_relu, g + 1)
                t = 0 if g < 2 else 1
                n = P if t == 0 else S
                o = sc[:, 0:P] if t == 0 else sc[:, P:3 * P]
                mask = causal[:, P:S] if t == 0 else causal[:, :]
                for i, h in enumerate(SCORE_HEADS[g]):
                    ins = dve.scalar_tensor_tensor(o, relu[:, g % 2, i * n:(i + 1) * n], wid[:, t, h:h + 1],
                                                   mask if h == 0 else o, ALU.mult, ALU.add)
                    if h == SCORE_HEADS[g][-1]:
                        ins.then_inc(s_racc, 1)
                        dve.wait_ge(s_racc, g + 1)
                    else:
                        link(ins)
            for t in range(TT):
                src = sc[:, 0:P] if t == 0 else sc[:, P:3 * P]
                dst = work[:, 0:P] if t == 0 else work[:, P:3 * P]
                for i in range(KEEP // 8):
                    link(dve.max(top[:, :], src))
                    link(dve.match_replace(dst, top[:, :], src, TAKEN))
                    src = dst
            link(dve.tensor_scalar(work[:, :], work[:, :], (TAKEN + FILL) / 2, -1e30, ALU.is_ge, ALU.mult))
            link(dve.tensor_tensor(work[:, 0:P], work[:, 0:P], causal[:, P:S], ALU.add))
            dve.tensor_tensor(work[:, P:3 * P], work[:, P:3 * P], causal[:, :], ALU.add).then_inc(s_mask, 1)

            def convolve(c):
                dve.wait_ge(s_actE, emptied_count(JOB_AT[("xr", c)])[1])
                for k in (2, 1, 0):
                    ins = dve.scalar_tensor_tensor(conv[:, c, :], xrnn[:, c, k:k + S], cw[:, k, c:c + 1], conv[:, c, :],
                                                   ALU.mult, ALU.add)
                    if k:
                        link(ins)
                ins.then_inc(s_conv, 1)

            for c in range(KC):
                convolve(c)
            dve.wait_ge(s_ckvTp, 1)
            for c in range(CC):
                dve.tensor_scalar(ckvT[:, c, :], ps[7][:, c * S:(c + 1) * S], kvn_sb[:, c:c + 1], None,
                                  ALU.mult).then_inc(s_ckvT, 1)
            dve.wait_ge(s_actE, emptied_count(JOB_AT[("lru", KC - 1)])[1])
            dve.wait_ge(s_conv, KC)
            dve.tensor_tensor(page(I_), page(I_), page(B_), ALU.mult).then_inc(s_conv, 1)
            dve.wait_ge(s_at, KC)
            dve.wait_ge(s_conv, KC + 1)
            link(dve.tensor_scalar(conv_tmp, page(R_), 1.0, None, ALU.add))
            link(dve.reciprocal(conv_tmp, conv_tmp))
            dve.tensor_tensor(page(R_), page(R_), conv_tmp, ALU.mult).then_inc(s_sqa, 1)
            dve.wait_ge(s_sqo, 1)
            link(dve.tensor_tensor(page(I_), page(I_), page(R_), ALU.mult))
            for c in range(KC):
                ins = dve.tensor_tensor_scan(rr[:, c, :], aa[:, c, :], ii[:, c, :], 0.0, ALU.mult, ALU.add)
                ins.then_inc(s_v, 1)
                chain[0] += 1
            dve.wait_ge(s_v, chain[0])
            dve.tensor_tensor(page(F_), page(F_), page(R_), ALU.mult).then_inc(s_y, 1)
            dve.wait_ge(s_y, 1)
            for i in range(4):
                dve.tensor_copy(v_sb[:, i // 2, (i % 2) * 512:(i % 2) * 512 + 512], job("v", i)[:, :]).then_inc(s_dveE, 1)

            def q_out(h):
                dve.tensor_scalar(q_sb[:, h, :], job("q", h)[:, 0:S], HD ** -0.5, None, ALU.mult).then_inc(s_dveE, 1)

            q_out(0)
            q_out(1)
            for h in range(HEADS):
                b = h % 2
                dve.wait_ge(s_lp, h + 1)
                dve.wait_ge(s_bm, h + 1)
                if h >= 2:
                    dve.wait_ge(s_ptp, h - 1)
                o = ps[4 + b]
                link(dve.tensor_tensor_reduce(lg[:, b, 0:P], o[:, 0:P], bm[:, b, 0:P], 1.0, -3.0e38, ALU.add, ALU.max,
                                              hst[:, b, 0:1]))
                ins = dve.tensor_tensor_reduce(lg[:, b, P:3 * P], o[:, P:3 * P], bm[:, b, P:3 * P], 1.0, -3.0e38,
                                               ALU.add, ALU.max, hst[:, b, 1:2])
                ins.then_inc(s_bmu, 1)
                dve.wait_ge(s_bmu, h + 1)
                dve.tensor_scalar(hst[:, b, 2:4], hst[:, b, 0:2], -1.0, None, ALU.mult).then_inc(s_lm, 1)
                if h + 2 < HEADS:
                    q_out(h + 2)
                dve.wait_ge(s_exp, 2 * h + 2)
                link(dve.reciprocal(hst[:, b, 6:8], hst[:, b, 4:6]))
                link(dve.tensor_scalar(lg[:, b, 0:P], lg[:, b, 0:P], hst[:, b, 6:7], None, ALU.mult))
                dve.tensor_scalar(lg[:, b, P:3 * P], lg[:, b, P:3 * P], hst[:, b, 7:8], None, ALU.mult).then_inc(s_pn, 1)
                dve.tensor_tensor(merged[:, h, :], job("pr", h)[:, 0:S], sig_r[:, h, :], ALU.mult).then_inc(s_dveE, 1)
            for c in range(KC):
                link(dve.tensor_tensor(tmpm, job("pa", c)[:, 0:S], sig_a[:, c, :], ALU.mult))
                dve.tensor_tensor(merged[:, c, :], merged[:, c, :], tmpm, ALU.add).then_inc(s_dveE, 1)
                dve.wait_ge(s_dveE, emptied_count(JOB_AT[("pa", c)])[1])

            def norm(t, zt, gv, bv, count):
                for f in range(2):
                    link(dve.bn_stats(stats[:, t, f, :], zt[:, f * 512:(f + 1) * 512]))
                link(dve.bn_aggr(mv[:, t, 0:2], stats[:, t, :, :].rearrange("p a b -> p (a b)")))
                dve.tensor_scalar(mv[:, t, 2:3], mv[:, t, 1:2], LN_EPS, None, ALU.add).then_inc(s_var, 1)
                dve.wait_ge(s_std, count)
                link(dve.reciprocal(mv[:, t, 3:4], mv[:, t, 2:3]))
                link(dve.tensor_scalar(zt, zt, mv[:, t, 0:1], mv[:, t, 3:4], ALU.subtract, ALU.mult))
                link(dve.tensor_tensor(zt, zt, gv, ALU.mult))
                return dve.tensor_tensor(zt, zt, bv, ALU.add)

            big = -3.0e38

            def route(t):
                r = rt[:, t, :]
                aff, sel, cho, gat = r[:, 0:16], r[:, 16:32], r[:, 32:48], r[:, 48:64]
                dve.wait_ge(s_aff, t + 1)
                link(dve.tensor_tensor(sel, aff, rb_sb[:, :], ALU.add))
                s4 = sel.rearrange("p (g e) -> p g e", e=PER_GROUP)
                hi, lo = r[:, 64:72].rearrange("p (g e) -> p g e", e=2), r[:, 72:80].rearrange("p (g e) -> p g e", e=2)
                link(dve.tensor_tensor(hi, s4[:, :, 0:2], s4[:, :, 2:4], ALU.max))
                link(dve.tensor_tensor(lo, s4[:, :, 0:2], s4[:, :, 2:4], ALU.min))
                gs = r[:, 80:88]
                link(dve.memset(gs, big))
                a4, b4, c4 = r[:, 88:92], gat[:, 0:4], gat[:, 4:8]
                link(dve.tensor_tensor(a4, hi[:, :, 0], hi[:, :, 1], ALU.max))
                link(dve.tensor_tensor(b4, hi[:, :, 0], hi[:, :, 1], ALU.min))
                link(dve.tensor_tensor(c4, lo[:, :, 0], lo[:, :, 1], ALU.max))
                link(dve.tensor_tensor(b4, b4, c4, ALU.max))
                link(dve.tensor_tensor(gs[:, 0:4], a4, b4, ALU.add))
                t8, i8 = r[:, 64:72], r[:, 72:80]
                link(dve.max(t8, gs))
                link(dve.max_index(i8.bitcast(U32), t8, gs))
                link(dve.tensor_copy(a4[:, 0:1], i8[:, 0:1].bitcast(U32)))
                link(dve.tensor_scalar(gat[:, 0:4], slot_no[:, 0:4], a4[:, 0:1], big, ALU.not_equal, ALU.mult))
                for g in range(GROUPS):
                    ins = dve.tensor_scalar(cho[:, 4 * g:4 * g + 4], sel[:, 4 * g:4 * g + 4], gat[:, g:g + 1], None, ALU.add)
                    link(ins)
                link(dve.max(t8, cho))
                link(dve.max_index(i8.bitcast(U32), t8, cho))
                link(dve.tensor_copy(a4[:, 0:2], i8[:, 0:2].bitcast(U32)))
                link(dve.tensor_scalar(gat, slot_no[:, 0:16], a4[:, 0:1], None, ALU.is_equal))
                link(dve.scalar_tensor_tensor(cho, slot_no[:, 0:16], a4[:, 1:2], gat, ALU.is_equal, ALU.add))
                link(dve.tensor_tensor(gat, cho, aff, ALU.mult))
                link(dve.tensor_reduce(a4[:, 2:3], gat, AX.X, ALU.add))
                link(dve.reciprocal(a4[:, 3:4], a4[:, 2:3]))
                dve.tensor_scalar(gat, gat, a4[:, 3:4], None, ALU.mult).then_inc(s_msk, 1)

            dve.wait_ge(s_x, 16)
            for t in range(TT):
                dve.wait_ge(s_wo, t + 1)
                for f in range(2):
                    link(dve.scalar_tensor_tensor(x1[:, t, f * 512:(f + 1) * 512], x_sb[:, t, f * 512:(f + 1) * 512], ALPHA,
                                                  ps[2 * t + f][:, :], ALU.mult, ALU.add))
                if t == 0:
                    dve.wait_ge(s_ln1, 32)
                norm(t, x1[:, t, :], lnv[:, 0, :], lnv[:, 1, :], t + 1).then_inc(s_x1, 1)
                dve.wait_ge(s_x1, t + 1)
                dve.tensor_scalar(acc[:, t, :], x1[:, t, :], ALPHA, None, ALU.mult).then_inc(s_v, 1)
                chain[0] += 1
                route(t)
            dve.wait_ge(s_pos, 1)
            dve.wait_ge(s_msk, TT)
            for t in range(TT):
                link(dve.scalar_tensor_tensor(rt[:, t, 64:80], ps[2][:, 16 * t:16 * t + 16], 1.0, rt[:, t, 32:48], ALU.add,
                                              ALU.mult))
                link(dve.tensor_scalar(rt[:, t, 64:80], rt[:, t, 64:80], -1.0, None, ALU.add))

            def one_hots(p, b):
                src = slot_no[:, SLOTS * b:SLOTS * (b + 1)].unsqueeze(1).to_broadcast([P, 2, SLOTS])
                for t in range(TT):
                    ins = dve.tensor_tensor(hot[:, t, :].rearrange("p (e s) -> p e s", e=2), src,
                                            rt[:, t, bass.ds(p * 2 + 64, 2)].unsqueeze(2).to_broadcast([P, 2, SLOTS]),
                                            ALU.is_equal)
                ins.then_inc(s_hot, 1)

            def gate_hots(p):
                for t in range(TT):
                    ins = dve.tensor_tensor(hotc[:, t, :].rearrange("p (e s) -> p e s", e=2),
                                            hot[:, t, :].rearrange("p (e s) -> p e s", e=2),
                                            rt[:, t, bass.ds(p * 2 + 48, 2)].unsqueeze(2).to_broadcast([P, 2, SLOTS]),
                                            ALU.mult)
                ins.then_inc(s_hotc, 1)

            one_hots(0, 0)
            dve.wait_ge(s_hot, 1)
            gate_hots(0)
            link(dve.tensor_reduce(cnt[:, 0:1], ps[2][:, 32:48], AX.X, ALU.max))
            for b in range(1, ROUNDS):
                link(dve.tensor_scalar(cnt[:, b:b + 1], cnt[:, 0:1], float(SLOTS * b), None, ALU.is_gt))
            dve.tensor_copy(cnt_i[:, :], cnt[:, :]).then_inc(s_cnt, 1)

            def pair(n, pn, bn):
                dve.wait_ge(s_xgp, n * 2 + 2)
                one_hots(pn, bn)
                dve.wait_ge(s_gp, n + 1)
                dve.tensor_copy(spread, ps[7][:, 0:S].rearrange("p (a b) -> p a b", a=TT)).then_inc(s_g, 1)
                dve.wait_ge(s_hot, n + 2)
                gate_hots(pn)
                for e in range(2):
                    dve.wait_ge(s_hp, n * 4 + (2 * e + 2))
                    dve.wait_ge(s_si, n * 2 + (e + 2))
                    dve.wait_ge(s_htp, n * 2 + (e + 1))
                    dve.tensor_tensor(he, ps[1][0:SLOTS, :], silu, ALU.mult).then_inc(s_he, 1)
                for i in range(4):
                    t, f = i // 2, i % 2
                    dve.wait_ge(s_sp4, n * 4 + (i + 2))
                    a = acc[:, t, f * 512:(f + 1) * 512]
                    dve.tensor_tensor(a, ps[7][:, :], a, ALU.add).then_inc(s_ac, 1)
                dve.wait_ge(s_ac, n * 4 + 5)

            def all_pairs(b):
                with dve.Fori(0, PAIRS - 1) as p:
                    pair(p + PAIRS * b, p + 1, b)
                pair(PAIRS * (b + 1) - 1, 0, b + 1)

            all_pairs(0)
            dve.wait_ge(s_cnt, 1)
            for b in range(1, ROUNDS):
                with dve.If(dve.value_load(cnt_i[0:1, b:b + 1], min_val=0, max_val=1)):
                    all_pairs(b)
            dve.wait_ge(s_ln2, 32)
            for t in range(TT):
                norm(t, acc[:, t, :], ln2v[:, 0, :], ln2v[:, 1, :], TT + t + 1).then_inc(s_fin, 1)


def laid_out(a):
    a = {k: np.ascontiguousarray(v) for k, v in a.items()}
    x, w_in = a["x"][0], a["w_in"][0]
    sizes = (1024, 1024, HEADS * HD, RANK, IDX_HEADS * IDX_DIM, IDX_DIM, IDX_HEADS, D, D)
    w_xr, w_g, w_q, w_ckv, w_qi, w_ki, w_wi, w_gr, w_ga = np.split(w_in, np.cumsum(sizes)[:-1], axis=1)

    def cols(w, c):
        return w[:, c * P:(c + 1) * P].reshape(KC, P, P).transpose(1, 0, 2).reshape(P, 1024)

    by_kind = {"ckv": w_ckv, "qidx": w_qi, "xr": w_xr, "g": w_g, "gr": w_gr, "ga": w_ga, "q": w_q,
               "pr": a["proj_rnn"][0], "pa": a["proj_att"][0], "kidx": np.concatenate([w_ki, w_ki], axis=1)}
    uk, uv = a["w_uk"][0], a["w_uv"][0]
    pieces = []
    for kind, c in PIECES:
        if kind == "uk":
            w = uk[4 * c:4 * c + 4].reshape(4, CC, P, HD).transpose(2, 0, 1, 3).reshape(P, 1024)
        elif kind == "uv":
            w = uv[:, c * P:(c + 1) * P, :].transpose(1, 0, 2).reshape(P, 1024)
        elif kind == "wo":
            w = a["w_out"][0][c * P:(c + 1) * P, :]
        else:
            w = cols(by_kind[kind], c)
        pieces.append(w)

    def features(v, n=KC):
        return v.reshape(n, P).T

    lru = np.stack([a["lru_wa"][0], a["lru_wx"][0]])
    lru = lru.reshape(2, KC, 2, 64, 64).transpose(2, 0, 3, 1, 4)
    dist = np.maximum(255 - np.arange(3 * P), 0)
    far = BUCKETS // 2 + (np.log(np.maximum(dist, 1).astype(np.float32) / (BUCKETS // 2))
                          / np.log(MAX_DIST / (BUCKETS // 2)) * (BUCKETS // 2)).astype(np.int32)
    bucket = np.where(dist < BUCKETS // 2, dist, np.minimum(far, BUCKETS - 1))
    g = {
        "x": x, "xT": x.T.reshape(KC, P, S).transpose(1, 0, 2), "wp": np.stack(pieces),
        "w_widx": w_wi.reshape(KC, P, IDX_HEADS).transpose(1, 0, 2),
        "conv_w": a["conv_w"][0].reshape(CONV, KC, P).transpose(2, 0, 1), "conv_b": features(a["conv_b"][0]),
        "lru_w": lru, "lru_ba": features(a["lru_ba"][0]), "lru_bx": features(a["lru_bx"][0]),
        "lam": features(a["lru_lambda"][0]), "kvn": features(a["kv_norm"][0], CC),
        "ln1_g": a["ln1_g"][0], "ln1_b": a["ln1_b"][0],
        "w_router": a["w_router"].reshape(KC, P, EXPERTS).transpose(1, 0, 2), "router_bias": a["router_bias"],
        "w_gate": a["exp_w_gate"][0].reshape(EXPERTS, KC, P, FF).transpose(0, 2, 1, 3).reshape(EXPERTS, P, KC * FF),
        "w_up": a["exp_w_up"][0].reshape(EXPERTS, KC, P, FF).transpose(0, 2, 1, 3).reshape(EXPERTS, P, KC * FF),
        "w_down": a["exp_w_down"][0].reshape(EXPERTS, FC, P, D).transpose(0, 2, 1, 3).reshape(EXPERTS, P, FC * D),
        "ln2_g": a["ln2_g"][0], "ln2_b": a["ln2_b"][0], "rel_bias": a["rel_bias"],
        "bucket_hot": (np.arange(BUCKETS)[:, None] == bucket[None]).astype(np.float32),
    }
    return {k: np.ascontiguousarray(v) for k, v in g.items()}


def kernel(**inputs):
    import concourse.bacc as bacc
    from concourse.bass_utils import run_bass_kernel_spmd

    nc = bacc.Bacc("TRN2", target_bir_lowering=False, num_devices=1)
    arrays = laid_out(inputs)
    args = [nc.dram_tensor(n, v.shape, mybir.dt.from_np(v.dtype), kind="ExternalInput").ap() for n, v in arrays.items()]
    args.append(nc.dram_tensor("out", [S, D], F32, kind="ExternalOutput").ap())
    hybrid_layer(nc, *args)
    r = run_bass_kernel_spmd(nc, [arrays], core_ids=[0])
    return r.results[0]["out"].reshape(1, S, D)
```

```python
from contextlib import ExitStack

import numpy as np

import concourse.bass as bass
from concourse import mybir

F32 = mybir.dt.float32
F32R = mybir.dt.float32r
I32 = mybir.dt.int32
U32 = mybir.dt.uint32
ALU = mybir.AluOpType
ACT = mybir.ActivationFunctionType
AX = mybir.AxisListType

P = 128
D = 1024
S = 256
KC = D // P
TT = S // P
HEADS = 8
HD = 128
RANK = 256
CC = RANK // P
IDX_HEADS = 8
IDX_DIM = 64
KEEP = 64
CONV = 4
LRU_C = 8.0
BUCKETS = 32
MAX_DIST = 128
EXPERTS = 16
GROUPS = 4
PER_GROUP = EXPERTS // GROUPS
FF = 512
FC = FF // P
ALPHA = 2.0 ** 0.25
LN_EPS = 1e-5
RMS_EPS = 1e-6
SLOTS = 64
PAIRS = EXPERTS // 2
ROUNDS = S // SLOTS
SUBS = 4
SUB = 1024
BY_VEC = SUBS - 1
U0, G1, D0, U1, G0_NEXT, D1 = 1, 2, 3, 4, 5, 6
PER_PAIR = 6
FILL = -3.0e38
TAKEN = -3.4e38
RING = 8
SPREAD_BANKS = (7, 2, 3, 4)
BANKS = 4


def mixer_pieces():
    out = [("ckv", 0), ("ckv", 1), ("kidx", 0)] + [("qidx", c) for c in range(4)]
    out += [("xr", c) for c in range(KC)] + [("g", c) for c in range(KC)]
    out += [("gr", c) for c in range(KC)] + [("ga", c) for c in range(KC)]
    out += [("uk", 0), ("uk", 1), ("uv", 0), ("uv", 1), ("q", 0), ("q", 1)]
    for h in range(HEADS):
        if h + 2 < HEADS:
            out.append(("q", h + 2))
        out.append(("pr", h))
    out += [("pa", c) for c in range(KC)] + [("wo", c) for c in range(KC)]
    return out


PIECES = mixer_pieces()
PIECE_AT = {key: i for i, key in enumerate(PIECES)}
LOADS = [(i, min(2, len(PIECES) - i)) for i in range(0, len(PIECES), 2)]


def mixer_jobs():
    out = [("ckv", 0), ("ckv", 1), ("kidx", 0)] + [("qidx", c) for c in range(4)]
    out += [(k, c) for k in ("xr", "g", "lru", "gr", "ga", "k") for c in range(KC)]
    out += [("v", i) for i in range(4)] + [("q", 0), ("q", 1)]
    for h in range(HEADS):
        if h + 2 < HEADS:
            out.append(("q", h + 2))
        out.append(("pr", h))
    return out + [("pa", c) for c in range(KC)]


JOBS = mixer_jobs()
JOB_AT = {key: j for j, key in enumerate(JOBS)}
SCORE_HEADS = [(0, 2, 4, 6), (1, 3, 5, 7), (0, 2), (1, 3), (4, 6), (5, 7)]
EARLY = (8, 11, 14, 17)
BY_DVE = {"ckv", "q", "v", "pr", "pa"}


def emptied_count(j):
    mine = JOBS[j][0] in BY_DVE
    return mine, sum((k in BY_DVE) == mine for k, _ in JOBS[:j + 1])


def jobs_to_free(i):
    kind, c = PIECES[i]
    last = {"ckv": ("ckv", 1), "uk": ("k", 4 * c + 3), "uv": ("v", 3)}.get(kind, (kind, c))
    return JOB_AT[last] + 1


def hybrid_layer(nc, x, xT, wp, w_widx, conv_w, conv_b, lru_w, lru_ba, lru_bx, lam, kvn, ln1_g, ln1_b,
                 w_router, router_bias, w_gate, w_up, w_down, ln2_g, ln2_b, rel_bias, bucket_hot, out):
    with ExitStack() as ctx:
        def sb(name, shape, dt=F32):
            return ctx.enter_context(nc.sbuf_tensor(name, shape, dt))

        def next_address():
            return -(-nc.sbuf_base // 32) * 32

        def sem(name):
            return ctx.enter_context(nc.semaphore(name))

        scratch = nc.dram_tensor("bias_scratch", [HEADS, 3 * P], F32, kind="Internal").ap()

        NPAGE = 10
        pages_at = next_address()
        pages = sb("pages", [P, NPAGE * 2048])
        A_, B_, I_, AP_, T_, XT_, S1_, S2_, R_, F_ = range(NPAGE)

        def page(i, n=1):
            return pages[:, i * 2048:(i + n) * 2048]

        def split(ap, **k):
            names = list(k)
            if len(names) == 1:
                return ap.rearrange("p (a b) -> p a b", a=k[names[0]])
            return ap.rearrange("p (a b c) -> p a b c", a=k[names[0]], b=k[names[1]])

        xrnn = sb("xrnn", [P, KC, S + CONV - 1])
        q_sb = split(page(A_), a=HEADS)
        x1 = split(page(A_), a=TT)
        conv = split(page(B_), a=KC)
        kT = split(page(B_), a=HEADS)
        acc = split(page(B_), a=TT)
        rr = split(page(R_), a=KC)
        merged = split(page(R_), a=KC)
        ii = split(page(I_), a=KC)
        v_sb = split(page(I_), a=TT)
        x1T = split(page(I_), a=KC)
        aa = split(page(AP_), a=KC)
        oT = split(page(AP_), a=HEADS)
        lruw = split(page(T_), a=KC, b=2)
        toep = split(page(T_), a=HEADS)
        lnv = split(page(T_), a=2)
        xT_sb = split(page(XT_), a=KC)
        x_sb = split(page(XT_), a=TT)
        sig_r = split(page(S1_), a=KC)
        sig_a = split(page(S2_), a=KC)
        qiT = split(pages[:, S1_ * 2048:S1_ * 2048 + 1024], a=4)
        kiT = pages[:, S1_ * 2048 + 1024:S1_ * 2048 + 1280]
        relu = split(pages[:, S2_ * 2048:S2_ * 2048 + 1024], a=2)
        gel = split(page(F_), a=KC)
        ring_at = next_address()
        ring = sb("ring", [P, RING, 1024])
        whi = nc.alloc_sbuf_tensor_at("whi", [P, SUBS, SUB], F32R, offset=ring_at)
        wlo = nc.alloc_sbuf_tensor_at("wlo", [P, SUBS, SUB], F32R, offset=ring_at + SUBS * SUB * 4)
        xs = nc.alloc_sbuf_tensor_at("xs", [P, 2, KC, 2, 2, SLOTS], F32R, offset=pages_at + I_ * 8192)
        ysb = page(T_)[:, 0:D]
        gsb = page(XT_)[0:SLOTS, 0:FF]
        usb = page(XT_)[0:SLOTS, FF:2 * FF]
        he = page(XT_)[0:SLOTS, 2 * FF:3 * FF]
        eg0 = sb("eg0", [P, KC * FF])
        eu0 = sb("eu0", [P, KC * FF])
        ed0 = sb("ed0", [P, FC * D])
        eg1 = sb("eg1", [P, KC * FF])
        ew = [(eg0[:, :], eu0[:, :], ed0[:, :]), (eg1[:, :], page(S1_, 2), page(R_, 2))]
        conv_tmp = page(A_)

        xrnn_flat = xrnn[:, :, :].rearrange("p a b -> p (a b)")[:, 0:2048]
        toep_rev = split(xrnn_flat, a=HEADS)
        ln2v = split(xrnn_flat, a=2)
        flip = sb("flip", [P, P])
        ident = sb("ident", [P, P])
        ones = sb("ones", [P, P])
        before = sb("before", [P, P])
        causal = sb("causal", [P, S])
        slot_no = sb("slot_no", [P, (ROUNDS + 1) * SLOTS])
        widx_w = sb("widx_w", [P, KC, IDX_HEADS])
        router_w = sb("router_w", [P, KC, EXPERTS])
        vec = sb("vec", [P, 9 * KC])
        cw = vec[:, 0:4 * KC].rearrange("p (a b) -> p a b", a=CONV)
        cb = vec[:, 4 * KC:5 * KC]
        ba = vec[:, 5 * KC:6 * KC]
        bx = vec[:, 6 * KC:7 * KC]
        lam_sb = vec[:, 7 * KC:8 * KC]
        kvn_sb = vec[:, 8 * KC:8 * KC + CC]
        sp = sb("sp", [P, 8, KC])
        rb_sb = sb("rb_sb", [P, EXPERTS])
        relb = sb("relb", [BUCKETS, HEADS])
        bvec = sb("bvec", [HEADS, 3 * P])
        ckv = sb("ckv", [P, TT, RANK])
        ckvT = sb("ckvT", [P, CC, S])
        wid = sb("wid", [P, TT, IDX_HEADS])
        stat = sb("stat", [P, 16])
        sc = sb("sc", [P, 3 * P])
        work = sb("work", [P, 3 * P])
        top = sb("top", [P, 8])
        bm = sb("bm", [P, 2, 3 * P])
        lg_at = next_address()
        lg = sb("lg", [P, 2, 3 * P])
        heS = nc.alloc_sbuf_tensor_at("heS", [P, FC, 2, SLOTS], F32R, offset=lg_at)
        moe_bm = bm[:, :, :].rearrange("p a b -> p (a b)")
        hot = split(moe_bm[:, 0:256], a=TT)
        hotc = split(moe_bm[:, 256:512], a=TT)
        spread = split(moe_bm[:, 512:768], a=TT)
        pT = sb("pT", [P, 3 * P])
        bhot = pT[0:BUCKETS, :]
        hst = sb("hst", [P, 2, 8])
        stats = sb("stats", [P, TT, 2, 6])
        mv = sb("mv", [P, TT, 4])
        rt = sb("rt", [P, TT, 96])
        cnt = sb("cnt", [P, 4])
        cnt_i = sb("cnt_i", [P, 4], I32)
        tmpm = lg[:, 0, 0:S]

        ps = [ctx.enter_context(nc.psum_tensor(f"ps{i}", [P, 512], F32)) for i in range(8)]

        s_small = sem("small_loaded")
        s_xT = sem("xT_loaded")
        s_lruw = sem("lruw_loaded")
        s_lruz = sem("lruw_zeroed")
        s_ring = [sem(f"ring_loaded{i}") for i in range(RING // 2)]
        s_x = sem("x_loaded")
        s_bvec = sem("bias_vector")
        s_bput = sem("bias_stored")
        s_toep = sem("toeplitz_loaded")
        s_tfp = sem("toeplitz_in_psum")
        s_tf = sem("toeplitz_ready")
        s_ln1 = sem("ln1_vectors")
        s_ln2 = sem("ln2_vectors")
        s_const = sem("constants")
        s_job = sem("job_done")
        s_actE = sem("emptied_by_act")
        s_dveE = sem("emptied_by_dve")
        s_sq = sem("ckv_squares")
        s_ms = sem("ckv_mean_squares")
        s_rms = sem("ckv_root")
        s_ckv = sem("ckv_ready")
        s_ckvTp = sem("ckvT_in_psum")
        s_ckvT = sem("ckvT_ready")
        s_scp = sem("scores_in_psum")
        s_relu = sem("relu_done")
        s_racc = sem("relu_used")
        s_bvp = sem("bias_in_psum")
        s_spe = sem("exp_lambda")
        s_sp = sem("softplus_ready")
        s_conv = sem("conv_ready")
        s_at = sem("decay_ready")
        s_sqa = sem("sqrt_arg")
        s_sqo = sem("sqrt_done")
        s_y = sem("y_rnn_ready")
        s_bm = sem("bias_mask_ready")
        s_bmu = sem("bias_mask_used")
        s_mask = sem("mask_ready")
        s_lp = sem("logits_in_psum")
        s_lm = sem("logits_max")
        s_exp = sem("exp_done")
        s_pn = sem("probs_ready")
        s_ptp = sem("probsT_in_psum")
        s_pt = sem("probsT_ready")
        s_op = sem("o_in_psum")
        s_o = sem("o_ready")
        s_wo = sem("mix_in_psum")
        s_var = sem("variance")
        s_std = sem("deviation")
        s_x1 = sem("x1_ready")
        s_x1Tp = sem("x1T_in_psum")
        s_x1T = sem("x1T_ready")
        s_rl = sem("router_in_psum")
        s_aff = sem("affinity")
        s_msk = sem("choice_ready")
        s_pos = sem("positions_in_psum")
        s_cnt = sem("count_ready")
        s_hot = sem("one_hot_ready")
        s_hotc = sem("gate_hot_ready")
        s_xgp = sem("gathered_in_psum")
        s_xg = sem("gathered_hi_ready")
        s_xgl = sem("gathered_lo_ready")
        s_wl = [[sem(f"w{'gud'[u]}{e}_loaded") for u in range(3)] for e in range(2)]
        s_hi = sem("weights_hi_ready")
        s_lo = sem("weights_lo_by_vector")
        s_lop = sem("weights_lo_by_pool")
        s_sub = sem("part_multiplied")
        s_fg = sem("gate_half_copied")
        s_gs = sem("gate_sum_ready")
        s_fu = sem("up_half_copied")
        s_us = sem("up_sum_ready")
        s_si = sem("silu_done")
        s_he = sem("hidden_ready")
        s_turn = sem("hidden_may_be_transposed")
        s_htp = sem("hiddenT_in_psum")
        s_ht = sem("hiddenT_hi_ready")
        s_htl = sem("hiddenT_lo_ready")
        s_ye = sem("y_half_copied")
        s_ys = sem("y_ready")
        s_gp = sem("spread_in_psum")
        s_g = sem("spread_ready")
        s_sp4 = sem("spread_out_in_psum")
        s_ac = sem("accumulated")
        s_fin = sem("result_ready")
        s_out = sem("result_stored")
        s_v = sem("vector_chain")
        s_a = sem("scalar_chain")
        s_p = sem("pool_chain")

        SMALL = 14
        block = ctx.enter_context(nc.Block())

        def piece(i):
            return ring[:, i % RING, :]

        def expert_ap(u, p, e):
            src = (w_gate, w_up, w_down)[u]
            return src[bass.ds(p * 2 + e, 1), :, :].rearrange("o p a -> (o p) a")

        @block.sync
        def _(sp_e):
            sp_e.dma_start(xT_sb, xT).then_inc(s_xT, 16)

            def ring_load(n):
                i, m = LOADS[n]
                if i >= RING:
                    sp_e.wait_ge(s_job, jobs_to_free(i + m - 1 - RING))
                sp_e.dma_start(ring[:, i % RING:i % RING + m, :],
                               wp[i:i + m, :, :].rearrange("a p b -> p a b")).then_inc(s_ring[n % 4], 16)

            ring_load(0)
            for dst, src in ((widx_w[:, :, :], w_widx), (cw, conv_w), (cb, conv_b), (ba, lru_ba), (bx, lru_bx),
                             (lam_sb, lam), (kvn_sb, kvn), (router_w[:, :, :], w_router), (relb[:, :], rel_bias),
                             (bhot, bucket_hot), (rb_sb[:, :], router_bias.partition_broadcast(P))):
                sp_e.dma_start(dst, src).then_inc(s_small, 16)
            for n in (1, 2, 3):
                ring_load(n)
            sp_e.wait_ge(s_lruz, 1)
            for par in range(2):
                for m in range(2):
                    sp_e.dma_start(lruw[64 * par:64 * par + 64, :, m, 64 * par:64 * par + 64],
                                   lru_w[par, m].rearrange("i c j -> i c j")).then_inc(s_lruw, 16)
            for n in range(4, len(LOADS)):
                ring_load(n)
                if n == 6:
                    sp_e.wait_ge(s_bvec, 1)
                    sp_e.dma_start(scratch, bvec[:, :]).then_inc(s_bput, 16)
                if n in EARLY:
                    e, u = divmod(EARLY.index(n), 3)
                    sp_e.dma_start(ew[e][u], expert_ap(u, 0, e)).then_inc(s_wl[e][u], 16)
                if LOADS[n][0] <= PIECE_AT[("gr", 2)] < LOADS[n][0] + 2:
                    sp_e.wait_ge(s_conv, KC)
                    sp_e.wait_ge(s_bput, 16)
                    sp_e.dma_start(toep_rev, bass.AP(tensor=scratch.tensor, offset=scratch.offset,
                                                     ap=[[1, P], [3 * P, HEADS], [1, S]])).then_inc(s_toep, 16)
                if LOADS[n][0] <= PIECE_AT[("wo", 0)] < LOADS[n][0] + 2:
                    sp_e.wait_ge(s_job, JOB_AT[("q", HEADS - 1)] + 1)
                    sp_e.dma_start(x_sb, x.rearrange("(t p) d -> p t d", p=P)).then_inc(s_x, 16)
                    sp_e.wait_ge(s_bm, HEADS)
                    sp_e.dma_start(lnv[:, 0, :], ln1_g.partition_broadcast(P)).then_inc(s_ln1, 16)
                    sp_e.dma_start(lnv[:, 1, :], ln1_b.partition_broadcast(P)).then_inc(s_ln1, 16)
            sp_e.wait_ge(s_dveE, emptied_count(JOB_AT[("pa", KC - 1)])[1])
            sp_e.dma_start(ew[1][1], expert_ap(1, 0, 1)).then_inc(s_wl[1][1], 16)
            sp_e.wait_ge(s_wo, 2)
            sp_e.dma_start(ew[1][2], expert_ap(2, 0, 1)).then_inc(s_wl[1][2], 16)
            sp_e.dma_start(ln2v[:, 0, :], ln2_g.partition_broadcast(P)).then_inc(s_ln2, 16)
            sp_e.dma_start(ln2v[:, 1, :], ln2_b.partition_broadcast(P)).then_inc(s_ln2, 16)

            def load_pair(n, p, g0, d1=D1):
                for e, u, place in ((0, 0, g0), (0, 1, U0), (1, 0, G1), (0, 2, D0), (1, 1, U1), (1, 2, d1)):
                    sp_e.wait_ge(s_sub, n * (SUBS * PER_PAIR) + SUBS * (place + 2))
                    sp_e.dma_start(ew[e][u], expert_ap(u, p, e)).then_inc(s_wl[e][u], 16)

            def load_round(b):
                load_pair(PAIRS * b, 1, 0)
                with sp_e.Fori(1, PAIRS - 1) as p:
                    load_pair(p + PAIRS * b, p + 1, -1)

            load_round(0)
            sp_e.wait_ge(s_cnt, 1)
            for b in range(1, ROUNDS):
                with sp_e.If(sp_e.value_load(cnt_i[0:1, b:b + 1], min_val=0, max_val=1)):
                    load_pair(PAIRS * b - 1, 0, -1, D1 - 1)
                    load_round(b)
            sp_e.wait_ge(s_fin, 1)
            sp_e.dma_start(out[0:P, :], acc[:, 0, :]).then_inc(s_out, 16)
            sp_e.wait_ge(s_fin, 2)
            sp_e.dma_start(out[P:S, :], acc[:, 1, :]).then_inc(s_out, 16)
            sp_e.wait_ge(s_out, 32)

        @block.gpsimd
        def _(pool):
            pool.memset(page(T_), 0.0).then_inc(s_lruz, 1)
            pool.memset(ident[:, :], 0.0).then_inc(s_p, 1)
            pool.memset(flip[:, :], 0.0).then_inc(s_p, 1)
            pool.memset(before[:, :], 1.0).then_inc(s_p, 1)
            pool.memset(causal[:, :], 0.0).then_inc(s_p, 1)
            pool.memset(ones[:, :], 1.0).then_inc(s_const, 1)
            pool.wait_ge(s_p, 4)
            pool.affine_select(out=flip[:, :], in_=flip[:, :], compare_op=ALU.not_equal, fill=1.0, base=1 - P,
                               pattern=[[1, P]], channel_multiplier=1).then_inc(s_const, 1)
            pool.affine_select(out=ident[:, :], in_=ident[:, :], compare_op=ALU.not_equal, fill=1.0, base=0,
                               pattern=[[-1, P]], channel_multiplier=1).then_inc(s_const, 1)
            pool.affine_select(out=before[:, :], in_=before[:, :], compare_op=ALU.is_gt, fill=0.0, base=0,
                               pattern=[[1, P]], channel_multiplier=-1).then_inc(s_const, 1)
            pool.affine_select(out=causal[:, :], in_=causal[:, :], compare_op=ALU.is_ge, fill=FILL, base=P,
                               pattern=[[-1, S]], channel_multiplier=1).then_inc(s_const, 1)
            pool.iota(slot_no[:, :], pattern=[[1, (ROUNDS + 1) * SLOTS]], base=0, channel_multiplier=0,
                      allow_small_or_imprecise_dtypes=True).then_inc(s_const, 1)
            pool.wait_ge(s_mask, 1)
            pool.wait_ge(s_tf, 4)
            for h in range(HEADS):
                if h >= 2:
                    pool.wait_ge(s_bmu, h - 1)
                pool.tensor_tensor(bm[:, h % 2, 0:P], toep[:, h, P:S], work[:, 0:P], ALU.add)
                pool.tensor_tensor(bm[:, h % 2, P:3 * P], toep[:, h, :], work[:, P:3 * P], ALU.add).then_inc(s_bm, 1)

            def low(n, e, u, place):
                r = SUBS - 1
                pool.wait_ge(s_hi, n * (SUBS * PER_PAIR) + (SUBS * place + r + 1))
                pool.tensor_tensor(wlo[:, r, :], ew[e][u][:, r * SUB:(r + 1) * SUB], whi[:, r, :].bitcast(F32),
                                   ALU.subtract).then_inc(s_lop, 1)

            def pair(n, last=False):
                low(n, 0, 1, U0)
                low(n, 1, 0, G1)
                low(n, 0, 2, D0)
                low(n, 1, 1, U1)
                if not last:
                    low(n, 0, 0, G0_NEXT)
                low(n, 1, 2, D1 - 1 if last else D1)

            def all_pairs(b):
                low(PAIRS * b, 0, 0, 0)
                pair(PAIRS * b)
                with pool.Fori(1, PAIRS - 1) as p:
                    pair(p + PAIRS * b)
                pair(PAIRS * (b + 1) - 1, True)

            all_pairs(0)
            pool.wait_ge(s_cnt, 1)
            for b in range(1, ROUNDS):
                with pool.If(pool.value_load(cnt_i[0:1, b:b + 1], min_val=0, max_val=1)):
                    all_pairs(b)

        @block.scalar
        def _(act):
            chain = [0]

            def link(ins):
                chain[0] += 1
                ins.then_inc(s_a, 1)
                act.wait_ge(s_a, chain[0])

            act.wait_ge(s_small, 11 * 16)
            link(act.activation(sp[:, 0, :], lam_sb, ACT.Abs))
            act.activation(sp[:, 1, :], sp[:, 0, :], ACT.Exp, scale=-1.0).then_inc(s_spe, 1)

            def job(kind, c):
                j = JOB_AT[(kind, c)]
                act.wait_ge(s_job, j + 1)
                return ps[j % BANKS]

            for t in range(TT):
                b = job("ckv", t)
                act.activation(lg[:, t, 0:RANK], b[:, 0:RANK], ACT.Square, accum_out=stat[:, t:t + 1]).then_inc(s_sq, 1)
            act.wait_ge(s_ms, 2)
            act.activation(stat[:, 4:6], stat[:, 2:4], ACT.Sqrt).then_inc(s_rms, 1)
            act.activation(kiT, job("kidx", 0)[:, 0:S], ACT.Copy).then_inc(s_actE, 1)
            for c in range(4):
                act.activation(qiT[:, c, :], job("qidx", c)[:, 0:S], ACT.Copy).then_inc(s_actE, 1)
            act.wait_ge(s_bvp, 1)
            act.activation(bvec[:, :], ps[6][0:HEADS, 0:3 * P], ACT.Copy).then_inc(s_bvec, 1)

            def x_rnn(c):
                b = job("xr", c)
                act.activation(xrnn[:, c, CONV - 1:], b[:, 0:S], ACT.Copy).then_inc(s_a, 1)
                chain[0] += 1
                act.activation(conv[:, c, :], b[:, 0:S], ACT.Identity, bias=cb[:, c:c + 1],
                               scale=cw[:, CONV - 1, c:c + 1]).then_inc(s_actE, 1)

            for g in range(6):
                act.wait_ge(s_scp, g + 1)
                if g >= 2:
                    act.wait_ge(s_racc, g - 1)
                act.activation(relu[:, g % 2, :], ps[4 + g % 2][:, :], ACT.Relu, scale=IDX_DIM ** -0.5).then_inc(s_relu, 1)
                x_rnn(g)
            x_rnn(6)
            x_rnn(7)
            for c in range(KC):
                act.activation(gel[:, c, :], job("g", c)[:, 0:S], ACT.Gelu_apprx_tanh).then_inc(s_actE, 1)
            for c in range(KC):
                b = job("lru", c)
                act.activation(rr[:, c, :], b[:, 0:S], ACT.Sigmoid, bias=ba[:, c:c + 1]).then_inc(s_a, 1)
                chain[0] += 1
                act.activation(ii[:, c, :], b[:, S:2 * S], ACT.Sigmoid, bias=bx[:, c:c + 1]).then_inc(s_actE, 1)
            act.wait_ge(s_racc, 6)
            for c in range(3):
                act.activation(sig_r[:, c, :], job("gr", c)[:, 0:S], ACT.Sigmoid).then_inc(s_actE, 1)
            act.wait_ge(s_sp, 1)
            act.wait_ge(s_a, chain[0])
            for c in range(KC):
                act.activation(aa[:, c, :], rr[:, c, :], ACT.Exp, scale=sp[:, 7, c:c + 1]).then_inc(s_a, 1)
                chain[0] += 1
            act.wait_ge(s_a, chain[0])
            for c in range(KC):
                act.activation(rr[:, c, :], rr[:, c, :], ACT.Tanh, scale=sp[:, 6, c:c + 1]).then_inc(s_at, 1)
            for c in range(3, KC):
                act.activation(sig_r[:, c, :], job("gr", c)[:, 0:S], ACT.Sigmoid).then_inc(s_actE, 1)
            for i in range(4):
                act.wait_ge(s_tfp, i + 1)
                act.activation(page(T_)[:, i * 512:(i + 1) * 512], ps[4 + i][:, :], ACT.Copy).then_inc(s_tf, 1)
            for c in range(4):
                act.activation(sig_a[:, c, :], job("ga", c)[:, 0:S], ACT.Sigmoid).then_inc(s_actE, 1)
            act.wait_ge(s_sqa, 1)
            act.activation(page(R_), page(R_), ACT.Sqrt, scale=2.0).then_inc(s_sqo, 1)
            for c in range(4, KC):
                act.activation(sig_a[:, c, :], job("ga", c)[:, 0:S], ACT.Sigmoid).then_inc(s_actE, 1)
            act.wait_ge(s_conv, KC + 1)
            for h in range(HEADS):
                act.activation(kT[:, h, :], job("k", h)[:, 0:S], ACT.Copy).then_inc(s_actE, 1)
            for h in range(HEADS + 1):
                if h < HEADS:
                    act.wait_ge(s_lm, h + 1)
                    b = h % 2
                    act.activation(lg[:, b, 0:P], lg[:, b, 0:P], ACT.Exp, bias=hst[:, b, 2:3],
                                   accum_out=hst[:, b, 4:5]).then_inc(s_exp, 1)
                    act.activation(lg[:, b, P:3 * P], lg[:, b, P:3 * P], ACT.Exp, bias=hst[:, b, 3:4],
                                   accum_out=hst[:, b, 5:6]).then_inc(s_exp, 1)
                if h >= 1:
                    act.wait_ge(s_ptp, h)
                    act.activation(pT[:, :], ps[6][:, 0:3 * P], ACT.Copy).then_inc(s_pt, 1)
                    act.wait_ge(s_op, h)
                    if h == 1:
                        act.wait_ge(s_y, 1)
                    act.activation(oT[:, h - 1, :], ps[7][:, 0:S], ACT.Copy).then_inc(s_o, 1)
            for t in range(TT):
                act.wait_ge(s_var, t + 1)
                act.activation(mv[:, t, 2:3], mv[:, t, 2:3], ACT.Sqrt).then_inc(s_std, 1)
                for k in range(2):
                    act.wait_ge(s_x1Tp, 2 * t + k + 1)
                    act.activation(x1T[:, 4 * k:4 * k + 4, t * P:(t + 1) * P], ps[4 + k][:, :].rearrange("p (a b) -> p a b", a=4),
                                   ACT.Copy).then_inc(s_x1T, 1)
                act.wait_ge(s_rl, t + 1)
                act.activation(rt[:, t, 0:EXPERTS], ps[6 + t][:, 0:EXPERTS], ACT.Sigmoid).then_inc(s_aff, 1)

            def high(n, e, u, place):
                act.wait_ge(s_wl[e][u], (n + 1 if place == G0_NEXT and (e, u) == (0, 0) else n) * 16 + 16)
                for r in range(SUBS):
                    act.wait_ge(s_sub, n * (SUBS * PER_PAIR) + (SUBS * place + r + 1))
                    act.activation(whi[:, r, :], ew[e][u][:, r * SUB:(r + 1) * SUB], ACT.Copy).then_inc(s_hi, 1)

            def product_done(n, place):
                act.wait_ge(s_sub, n * (SUBS * PER_PAIR) + SUBS * (place + 2))

            def gathered(n, k, par):
                act.wait_ge(s_xgp, n * 2 + (k + 1))
                for e in range(2):
                    ins = act.activation(xs[:, par, 4 * k:4 * k + 4, e, 0, :],
                                         ps[3 + k][:, :].rearrange("p (a e s) -> p a e s", a=4, e=2)[:, :, e, :], ACT.Copy)
                ins.then_inc(s_xg, 1)

            def gate_half(n, e, place):
                product_done(n, place)
                m = n + 1 if place == G0_NEXT else n
                act.wait_ge(s_he, m * 2 + (e + 1))
                act.activation(gsb, ps[0][SLOTS:P, :], ACT.Copy).then_inc(s_fg, 1)

            def up_half(n, e, place):
                product_done(n, place)
                act.wait_ge(s_he, n * 2 + (e + 1))
                act.activation(usb, ps[1][SLOTS:P, :], ACT.Copy).then_inc(s_fu, 1)

            def silu(n, e):
                act.wait_ge(s_gs, n * 2 + (e + 2))
                act.activation(gsb, gsb, ACT.Silu).then_inc(s_si, 1)

            def hidden_T(n, e):
                act.wait_ge(s_htp, n * 2 + (e + 2))
                act.activation(heS[:, :, 0, :], ps[2][:, 0:FC * SLOTS].rearrange("p (a b) -> p a b", a=FC),
                               ACT.Copy).then_inc(s_ht, 1)

            def y_half(n, e, place):
                product_done(n, place)
                act.wait_ge(s_sp4, n * 4 + 1)
                for f in range(2):
                    act.activation(ysb[64 * e:64 * e + 64, f * 512:(f + 1) * 512],
                                   ps[5 + f][64 - 64 * e:128 - 64 * e, :], ACT.Copy).then_inc(s_ye, 1)

            def pair(n, par, first=False, last=False):
                high(n, 0, 1, U0)
                if not first:
                    y_half(n - 1, 1, D1)
                silu(n, 0)
                high(n, 1, 0, G1)
                up_half(n, 0, U0)
                gathered(n + 1, 0, 1 - par)
                high(n, 0, 2, D0)
                gate_half(n, 1, G1)
                hidden_T(n, 0)
                gathered(n + 1, 1, 1 - par)
                high(n, 1, 1, U1)
                y_half(n, 0, D0)
                silu(n, 1)
                if not last:
                    high(n, 0, 0, G0_NEXT)
                up_half(n, 1, U1)
                high(n, 1, 2, D1 - 1 if last else D1)
                if not last:
                    gate_half(n, 0, G0_NEXT)
                hidden_T(n, 1)
                if last:
                    y_half(n, 1, D1 - 1)

            def all_pairs(b):
                n = PAIRS * b
                high(n, 0, 0, 0)
                if b == 0:
                    gathered(0, 0, 0)
                    gathered(0, 1, 0)
                gate_half(n, 0, 0)
                pair(n, 0, first=True)
                with act.Fori(1, PAIRS - 1, 2) as p:
                    pair(p + n, 1)
                    pair(p + (n + 1), 0)
                pair(n + PAIRS - 1, 1, last=True)

            act.wait_ge(s_wo, TT)
            all_pairs(0)
            for b in range(1, ROUNDS):
                with act.If(act.value_load(cnt_i[0:1, b:b + 1], min_val=0, max_val=1)):
                    all_pairs(b)
            for t in range(TT):
                act.wait_ge(s_var, TT + t + 1)
                act.activation(mv[:, t, 2:3], mv[:, t, 2:3], ACT.Sqrt).then_inc(s_std, 1)

        @block.tensor
        def _(pe):
            def need(kind, c):
                i = PIECE_AT[(kind, c)]
                n = i // 2
                pe.wait_ge(s_ring[n % 4], 16 * (n // 4 + 1))
                return piece(i)

            def start_job(kind, c):
                j = JOB_AT[(kind, c)]
                if j >= BANKS:
                    by_dve, n = emptied_count(j - BANKS)
                    pe.wait_ge(s_dveE if by_dve else s_actE, n)
                return ps[j % BANKS]

            for free, count in ((s_htp, 1), (s_sp4, 1), (s_sub, SUBS)):
                pe.sem_inc(free, count)
            pe.wait_ge(s_xT, 16)
            for c in range(CC):
                w = need("ckv", c).rearrange("p (k n) -> p k n", k=KC)
                for t in range(TT):
                    for k in range(KC):
                        ins = pe.matmul(ps[t][:, c * P:(c + 1) * P], xT_sb[:, k, t * P:(t + 1) * P], w[:, k, :],
                                        start=(k == 0), stop=(k == KC - 1))
            pe.wait_ge(s_small, 11 * 16)
            for t in range(TT):
                for k in range(KC):
                    ins = pe.matmul(ps[t][:, RANK:RANK + IDX_HEADS], xT_sb[:, k, t * P:(t + 1) * P], widx_w[:, k, :],
                                    start=(k == 0), stop=(k == KC - 1))
                ins.then_inc(s_job, 1)

            def plain(kind, c, rhs, wait=None):
                w = need(kind, c)
                o = start_job(kind, c)
                if wait:
                    pe.wait_ge(*wait)
                for k in range(KC):
                    ins = pe.matmul(o[:, 0:S], w[:, k * P:(k + 1) * P], rhs[:, k, :], start=(k == 0), stop=(k == KC - 1))
                ins.then_inc(s_job, 1)

            plain("kidx", 0, xT_sb)
            for c in range(4):
                plain("qidx", c, xT_sb)
            pe.matmul(ps[6][0:HEADS, 0:3 * P], relb[:, :], bhot, start=True, stop=True).then_inc(s_bvp, 1)

            pe.wait_ge(s_actE, 5)

            def scores(g):
                if g >= 2:
                    pe.wait_ge(s_relu, g - 1)
                t = 0 if g < 2 else 1
                n = P if t == 0 else S
                for i, h in enumerate(SCORE_HEADS[g]):
                    r = 64 * (h % 2)
                    ins = pe.matmul(ps[4 + g % 2][:, i * n:(i + 1) * n], qiT[r:r + 64, h // 2, t * P:(t + 1) * P],
                                    kiT[r:r + 64, 0:n], start=True, stop=True)
                ins.then_inc(s_scp, 1)

            for c in range(KC):
                if c < 6:
                    scores(c)
                plain("xr", c, xT_sb)
            pe.wait_ge(s_const, 6)
            pe.wait_ge(s_ckv, TT)
            for c in range(CC):
                for t in range(TT):
                    ins = pe.transpose(ps[7][:, c * S + t * P:c * S + (t + 1) * P], ckv[:, t, c * P:(c + 1) * P], ident[:, :])
            ins.then_inc(s_ckvTp, 1)
            for c in range(KC):
                plain("g", c, xT_sb)
            pe.wait_ge(s_lruw, 64)
            for c in range(KC):
                o = start_job("lru", c)
                pe.wait_ge(s_conv, c + 1)
                for m in range(2):
                    ins = pe.matmul(o[:, m * S:(m + 1) * S], lruw[:, c, m, :], conv[:, c, :], start=True, stop=True)
                ins.then_inc(s_job, 1)
            for c in range(KC):
                plain("gr", c, xT_sb)
            pe.wait_ge(s_toep, 16)
            pe.wait_ge(s_relu, 6)
            pe.wait_ge(s_bvec, 1)
            pe.wait_ge(s_ckvT, 2)
            for i in range(4):
                pe.matmul(ps[4 + i][:, :], flip[:, :], xrnn_flat[:, i * 512:(i + 1) * 512], start=True,
                          stop=True).then_inc(s_tfp, 1)
            for c in range(KC):
                plain("ga", c, xT_sb)
            pe.wait_ge(s_ckvT, 2)
            for h in range(HEADS):
                w = need("uk", h // 4).rearrange("p (h c d) -> p h c d", h=4, c=CC)
                o = start_job("k", h)
                for c in range(CC):
                    ins = pe.matmul(o[:, 0:S], w[:, h % 4, c, :], ckvT[:, c, :], start=(c == 0), stop=(c == CC - 1))
                ins.then_inc(s_job, 1)
            wv = [need("uv", c) for c in range(CC)]
            for i in range(4):
                t, f = i // 2, i % 2
                o = start_job("v", i)
                for c in range(CC):
                    ins = pe.matmul(o[:, :], ckvT[:, c, t * P:(t + 1) * P], wv[c][:, f * 512:(f + 1) * 512],
                                    start=(c == 0), stop=(c == CC - 1))
                ins.then_inc(s_job, 1)
            plain("q", 0, xT_sb)
            plain("q", 1, xT_sb)

            def logits(h):
                pe.wait_ge(s_dveE, emptied_count(JOB_AT[("q", h)])[1])
                pe.wait_ge(s_actE, emptied_count(JOB_AT[("k", h)])[1])
                if h >= 2:
                    pe.wait_ge(s_lm, h - 1)
                o = ps[4 + h % 2]
                pe.matmul(o[:, 0:P], q_sb[:, h, 0:P], kT[:, h, 0:P], start=True, stop=True)
                pe.matmul(o[:, P:3 * P], q_sb[:, h, P:S], kT[:, h, :], start=True, stop=True).then_inc(s_lp, 1)

            def probs_T(h):
                pe.wait_ge(s_pn, h + 1)
                if h >= 1:
                    pe.wait_ge(s_pt, h)
                for i in range(3):
                    ins = pe.transpose(ps[6][:, i * P:(i + 1) * P], lg[:, h % 2, i * P:(i + 1) * P], ident[:, :])
                ins.then_inc(s_ptp, 1)

            def values(h):
                pe.wait_ge(s_pt, h + 1)
                if h >= 1:
                    pe.wait_ge(s_o, h)
                pe.matmul(ps[7][:, 0:S], v_sb[:, 0, h * HD:(h + 1) * HD], pT[:, 0:S], start=True, stop=False)
                pe.matmul(ps[7][:, P:S], v_sb[:, 1, h * HD:(h + 1) * HD], pT[:, S:3 * P], start=False,
                          stop=True).then_inc(s_op, 1)

            for h in range(HEADS + 1):
                if h < HEADS:
                    logits(h)
                if h + 2 < HEADS:
                    plain("q", h + 2, xT_sb)
                if h >= 1:
                    probs_T(h - 1)
                if h < HEADS:
                    plain("pr", h, gel, (s_y, 1))
                if h >= 1:
                    values(h - 1)
            for c in range(KC):
                plain("pa", c, oT, (s_o, HEADS))

            last = emptied_count(JOB_AT[("pa", KC - 1)])[1]
            pe.wait_ge(s_dveE, last)
            for k in range(0, KC, 1):
                need("wo", k)
            for t in range(TT):
                for f in range(2):
                    for k in range(KC):
                        ins = pe.matmul(ps[2 * t + f][:, :], merged[:, k, t * P:(t + 1) * P],
                                        piece(PIECE_AT[("wo", k)])[:, f * 512:(f + 1) * 512],
                                        start=(k == 0), stop=(k == KC - 1))
                ins.then_inc(s_wo, 1)

            for t in range(TT):
                pe.wait_ge(s_x1, t + 1)
                for k in range(2):
                    if t >= 1:
                        pe.wait_ge(s_x1T, 2 * t - 1 + k)
                    for i in range(4):
                        ins = pe.transpose(ps[4 + k][:, i * P:(i + 1) * P],
                                           x1[:, t, (4 * k + i) * P:(4 * k + i + 1) * P], ident[:, :])
                    ins.then_inc(s_x1Tp, 1)
                pe.wait_ge(s_x1T, 2 * t + 2)
                for k in range(KC):
                    ins = pe.matmul(ps[6 + t][:, 0:EXPERTS], x1T[:, k, t * P:(t + 1) * P], router_w[:, k, :],
                                    start=(k == 0), stop=(k == KC - 1))
                ins.then_inc(s_rl, 1)
            pe.wait_ge(s_msk, TT)
            m0, m1 = rt[:, 0, 32:48], rt[:, 1, 32:48]
            pe.matmul(ps[2][:, 0:16], before[:, :], m0, start=True, stop=True)
            pe.matmul(ps[2][:, 16:32], ones[:, :], m0, start=True, stop=False)
            pe.matmul(ps[2][:, 16:32], before[:, :], m1, start=False, stop=True)
            pe.matmul(ps[2][:, 32:48], ones[:, :], m0, start=True, stop=False)
            pe.matmul(ps[2][:, 32:48], ones[:, :], m1, start=False, stop=True).then_inc(s_pos, 1)

            def gather(k):
                for i in range(4):
                    for t in range(TT):
                        ins = pe.matmul(ps[3 + k][:, i * P:(i + 1) * P],
                                        x1[:, t, (4 * k + i) * P:(4 * k + i + 1) * P], hot[:, t, :],
                                        start=(t == 0), stop=(t == TT - 1))
                ins.then_inc(s_xgp, 1)

            def gather_next(n, k):
                pe.wait_ge(s_hot, n + 2)
                pe.wait_ge(s_xgl, n * 2 + (k + 2))
                pe.wait_ge(s_ac, n * 4 + 1)
                gather(k)

            def parts(n, place):
                for r in range(SUBS):
                    if r < BY_VEC:
                        pe.wait_ge(s_lo, n * (BY_VEC * PER_PAIR) + (BY_VEC * place + r + 1))
                    else:
                        pe.wait_ge(s_lop, n * PER_PAIR + (place + 1))
                    yield r

            def hidden(n, e, u, place, par):
                m = n + 1 if place == G0_NEXT else n
                pe.wait_ge(s_xgl, m * 2 + 3)
                pe.wait_ge(s_us if u else s_gs, m * 2 + (e + 1))
                for r in parts(n, place):
                    for k in (2 * r, 2 * r + 1):
                        for part in (whi, wlo):
                            ins = pe.matmul(ps[u][:, :], xs[:, par, k, e, :, :].rearrange("p a b -> p (a b)"),
                                            part[:, r, (k % 2) * FF:(k % 2 + 1) * FF],
                                            start=(k == 0 and part is whi), stop=(k == KC - 1 and part is wlo))
                    ins.then_inc(s_sub, 1)

            def hidden_T(n, e):
                pe.wait_ge(s_he, n * 2 + (e + 2))
                pe.wait_ge(s_htl, n * 2 + (e + 1))
                pe.wait_ge(s_ac, n * 4 + 1)
                pe.sem_inc(s_turn, 1)
                for f in range(FC):
                    ins = pe.transpose(ps[2][:, f * SLOTS:(f + 1) * SLOTS], he[:, f * P:(f + 1) * P],
                                       ident[0:SLOTS, 0:SLOTS])
                ins.then_inc(s_htp, 1)

            def down(n, e, place):
                pe.wait_ge(s_htl, n * 2 + (e + 2))
                pe.wait_ge(s_ys, n * 4 + (2 * e + 1))
                for r in parts(n, place):
                    for f in range(2):
                        for part in (whi, wlo):
                            ins = pe.matmul(ps[5 + f][:, :], heS[:, r, :, :].rearrange("p a b -> p (a b)"),
                                            part[:, r, f * 512:(f + 1) * 512],
                                            start=(r == 0 and part is whi), stop=(r == FC - 1 and part is wlo))
                    ins.then_inc(s_sub, 1)

            def spread_T(n):
                pe.wait_ge(s_hotc, n + 1)
                pe.wait_ge(s_ac, n * 4 + 1)
                for t in range(TT):
                    ins = pe.transpose(ps[7][:, t * P:(t + 1) * P], hotc[:, t, :], ident[:, :])
                ins.then_inc(s_gp, 1)

            def spread_out(n):
                pe.wait_ge(s_g, n + 1)
                pe.wait_ge(s_ys, n * 4 + 5)
                pe.wait_ge(s_htl, n * 2 + 3)
                pe.wait_ge(s_xgl, n * 2 + 5)
                for i, bank in enumerate(SPREAD_BANKS):
                    t, f = i // 2, i % 2
                    pe.matmul(ps[bank][:, :], spread[:, t, :], ysb[:, f * 512:(f + 1) * 512], start=True,
                              stop=True).then_inc(s_sp4, 1)

            def pair(n, par, first=False, last=False):
                hidden(n, 0, 1, U0, par)
                if not first:
                    spread_out(n - 1)
                hidden(n, 1, 0, G1, par)
                gather_next(n, 0)
                hidden_T(n, 0)
                gather_next(n, 1)
                down(n, 0, D0)
                hidden(n, 1, 1, U1, par)
                if not last:
                    hidden(n, 0, 0, G0_NEXT, 1 - par)
                hidden_T(n, 1)
                spread_T(n)
                down(n, 1, D1 - 1 if last else D1)
                if last:
                    spread_out(n)

            def all_pairs(b):
                n = PAIRS * b
                hidden(n, 0, 0, 0, 0)
                pair(n, 0, first=True)
                with pe.Fori(1, PAIRS - 1, 2) as p:
                    pair(p + n, 1)
                    pair(p + (n + 1), 0)
                pair(n + PAIRS - 1, 1, last=True)

            pe.wait_ge(s_hot, 1)
            gather(0)
            gather(1)
            all_pairs(0)
            for b in range(1, ROUNDS):
                with pe.If(pe.value_load(cnt_i[0:1, b:b + 1], min_val=0, max_val=1)):
                    all_pairs(b)

        @block.vector
        def _(dve):
            chain = [0]

            def link(ins):
                chain[0] += 1
                ins.then_inc(s_v, 1)
                dve.wait_ge(s_v, chain[0])

            def job(kind, c):
                j = JOB_AT[(kind, c)]
                dve.wait_ge(s_job, j + 1)
                return ps[j % BANKS]

            for free in (s_he, s_ac, s_gs, s_us, s_htl, s_xgl, s_ys):
                dve.sem_inc(free, 1)
            link(dve.memset(xrnn[:, :, 0:CONV - 1], 0.0))
            dve.wait_ge(s_spe, 1)
            z, w, w2, h_ = sp[:, 1, :], sp[:, 2, :], sp[:, 3, :], sp[:, 4, :]
            link(dve.tensor_scalar(w, z, 2.0, None, ALU.add))
            link(dve.reciprocal(w, w))
            link(dve.tensor_tensor(w, w, z, ALU.mult))
            link(dve.tensor_tensor(w2, w, w, ALU.mult))
            link(dve.tensor_scalar(h_, w2, 1.0 / 17, 1.0 / 15, ALU.mult, ALU.add))
            for d in (13, 11, 9, 7, 5, 3, 1):
                link(dve.tensor_tensor(h_, h_, w2, ALU.mult))
                link(dve.tensor_scalar(h_, h_, 1.0 / d, None, ALU.add))
            link(dve.tensor_tensor(h_, h_, w, ALU.mult))
            link(dve.tensor_scalar(sp[:, 5, :], lam_sb, -1.0, 0.0, ALU.mult, ALU.max))
            link(dve.scalar_tensor_tensor(sp[:, 5, :], h_, 2.0, sp[:, 5, :], ALU.mult, ALU.add))
            link(dve.tensor_scalar(sp[:, 6, :], sp[:, 5, :], LRU_C, None, ALU.mult))
            dve.tensor_scalar(sp[:, 7, :], sp[:, 5, :], -LRU_C, None, ALU.mult).then_inc(s_sp, 1)

            for t in range(TT):
                dve.wait_ge(s_sq, t + 1)
                dve.tensor_scalar(stat[:, 2 + t:3 + t], stat[:, t:t + 1], 1.0 / RANK, RMS_EPS, ALU.mult,
                                  ALU.add).then_inc(s_ms, 1)
            dve.wait_ge(s_rms, 1)
            link(dve.reciprocal(stat[:, 6:8], stat[:, 4:6]))
            for t in range(TT):
                b = job("ckv", t)
                dve.tensor_scalar(ckv[:, t, :], b[:, 0:RANK], stat[:, 6 + t:7 + t], None, ALU.mult).then_inc(s_ckv, 1)
                dve.tensor_scalar(wid[:, t, :], b[:, RANK:RANK + IDX_HEADS], IDX_HEADS ** -0.5, None,
                                  ALU.mult).then_inc(s_dveE, 1)
            dve.wait_ge(s_dveE, 2)
            dve.wait_ge(s_const, 6)
            for g in range(6):
                dve.wait_ge(s_relu, g + 1)
                t = 0 if g < 2 else 1
                n = P if t == 0 else S
                o = sc[:, 0:P] if t == 0 else sc[:, P:3 * P]
                mask = causal[:, P:S] if t == 0 else causal[:, :]
                for i, h in enumerate(SCORE_HEADS[g]):
                    ins = dve.scalar_tensor_tensor(o, relu[:, g % 2, i * n:(i + 1) * n], wid[:, t, h:h + 1],
                                                   mask if h == 0 else o, ALU.mult, ALU.add)
                    if h == SCORE_HEADS[g][-1]:
                        ins.then_inc(s_racc, 1)
                        dve.wait_ge(s_racc, g + 1)
                    else:
                        link(ins)
            for t in range(TT):
                src = sc[:, 0:P] if t == 0 else sc[:, P:3 * P]
                dst = work[:, 0:P] if t == 0 else work[:, P:3 * P]
                for i in range(KEEP // 8):
                    link(dve.max(top[:, :], src))
                    link(dve.match_replace(dst, top[:, :], src, TAKEN))
                    src = dst
            link(dve.tensor_scalar(work[:, :], work[:, :], (TAKEN + FILL) / 2, -1e30, ALU.is_ge, ALU.mult))
            link(dve.tensor_tensor(work[:, 0:P], work[:, 0:P], causal[:, P:S], ALU.add))
            dve.tensor_tensor(work[:, P:3 * P], work[:, P:3 * P], causal[:, :], ALU.add).then_inc(s_mask, 1)

            def convolve(c):
                dve.wait_ge(s_actE, emptied_count(JOB_AT[("xr", c)])[1])
                for k in (2, 1, 0):
                    ins = dve.scalar_tensor_tensor(conv[:, c, :], xrnn[:, c, k:k + S], cw[:, k, c:c + 1], conv[:, c, :],
                                                   ALU.mult, ALU.add)
                    if k:
                        link(ins)
                ins.then_inc(s_conv, 1)

            for c in range(KC):
                convolve(c)
            dve.wait_ge(s_ckvTp, 1)
            for c in range(CC):
                dve.tensor_scalar(ckvT[:, c, :], ps[7][:, c * S:(c + 1) * S], kvn_sb[:, c:c + 1], None,
                                  ALU.mult).then_inc(s_ckvT, 1)
            dve.wait_ge(s_actE, emptied_count(JOB_AT[("lru", KC - 1)])[1])
            dve.wait_ge(s_conv, KC)
            dve.tensor_tensor(page(I_), page(I_), page(B_), ALU.mult).then_inc(s_conv, 1)
            dve.wait_ge(s_at, KC)
            dve.wait_ge(s_conv, KC + 1)
            link(dve.tensor_scalar(conv_tmp, page(R_), 1.0, None, ALU.add))
            link(dve.reciprocal(conv_tmp, conv_tmp))
            dve.tensor_tensor(page(R_), page(R_), conv_tmp, ALU.mult).then_inc(s_sqa, 1)
            dve.wait_ge(s_sqo, 1)
            link(dve.tensor_tensor(page(I_), page(I_), page(R_), ALU.mult))
            for c in range(KC):
                ins = dve.tensor_tensor_scan(rr[:, c, :], aa[:, c, :], ii[:, c, :], 0.0, ALU.mult, ALU.add)
                ins.then_inc(s_v, 1)
                chain[0] += 1
            dve.wait_ge(s_v, chain[0])
            dve.tensor_tensor(page(F_), page(F_), page(R_), ALU.mult).then_inc(s_y, 1)
            dve.wait_ge(s_y, 1)
            for i in range(4):
                dve.tensor_copy(v_sb[:, i // 2, (i % 2) * 512:(i % 2) * 512 + 512], job("v", i)[:, :]).then_inc(s_dveE, 1)

            def q_out(h):
                dve.tensor_scalar(q_sb[:, h, :], job("q", h)[:, 0:S], HD ** -0.5, None, ALU.mult).then_inc(s_dveE, 1)

            q_out(0)
            q_out(1)
            for h in range(HEADS):
                b = h % 2
                dve.wait_ge(s_lp, h + 1)
                dve.wait_ge(s_bm, h + 1)
                if h >= 2:
                    dve.wait_ge(s_ptp, h - 1)
                o = ps[4 + b]
                link(dve.tensor_tensor_reduce(lg[:, b, 0:P], o[:, 0:P], bm[:, b, 0:P], 1.0, -3.0e38, ALU.add, ALU.max,
                                              hst[:, b, 0:1]))
                ins = dve.tensor_tensor_reduce(lg[:, b, P:3 * P], o[:, P:3 * P], bm[:, b, P:3 * P], 1.0, -3.0e38,
                                               ALU.add, ALU.max, hst[:, b, 1:2])
                ins.then_inc(s_bmu, 1)
                dve.wait_ge(s_bmu, h + 1)
                dve.tensor_scalar(hst[:, b, 2:4], hst[:, b, 0:2], -1.0, None, ALU.mult).then_inc(s_lm, 1)
                if h + 2 < HEADS:
                    q_out(h + 2)
                dve.wait_ge(s_exp, 2 * h + 2)
                link(dve.reciprocal(hst[:, b, 6:8], hst[:, b, 4:6]))
                link(dve.tensor_scalar(lg[:, b, 0:P], lg[:, b, 0:P], hst[:, b, 6:7], None, ALU.mult))
                dve.tensor_scalar(lg[:, b, P:3 * P], lg[:, b, P:3 * P], hst[:, b, 7:8], None, ALU.mult).then_inc(s_pn, 1)
                dve.tensor_tensor(merged[:, h, :], job("pr", h)[:, 0:S], sig_r[:, h, :], ALU.mult).then_inc(s_dveE, 1)
            for c in range(KC):
                link(dve.tensor_tensor(tmpm, job("pa", c)[:, 0:S], sig_a[:, c, :], ALU.mult))
                dve.tensor_tensor(merged[:, c, :], merged[:, c, :], tmpm, ALU.add).then_inc(s_dveE, 1)
                dve.wait_ge(s_dveE, emptied_count(JOB_AT[("pa", c)])[1])

            def norm(t, zt, gv, bv, count):
                for f in range(2):
                    link(dve.bn_stats(stats[:, t, f, :], zt[:, f * 512:(f + 1) * 512]))
                link(dve.bn_aggr(mv[:, t, 0:2], stats[:, t, :, :].rearrange("p a b -> p (a b)")))
                dve.tensor_scalar(mv[:, t, 2:3], mv[:, t, 1:2], LN_EPS, None, ALU.add).then_inc(s_var, 1)
                dve.wait_ge(s_std, count)
                link(dve.reciprocal(mv[:, t, 3:4], mv[:, t, 2:3]))
                link(dve.tensor_scalar(zt, zt, mv[:, t, 0:1], mv[:, t, 3:4], ALU.subtract, ALU.mult))
                link(dve.tensor_tensor(zt, zt, gv, ALU.mult))
                return dve.tensor_tensor(zt, zt, bv, ALU.add)

            big = -3.0e38

            def route(t):
                r = rt[:, t, :]
                aff, sel, cho, gat = r[:, 0:16], r[:, 16:32], r[:, 32:48], r[:, 48:64]
                dve.wait_ge(s_aff, t + 1)
                link(dve.tensor_tensor(sel, aff, rb_sb[:, :], ALU.add))
                s4 = sel.rearrange("p (g e) -> p g e", e=PER_GROUP)
                hi, lo = r[:, 64:72].rearrange("p (g e) -> p g e", e=2), r[:, 72:80].rearrange("p (g e) -> p g e", e=2)
                link(dve.tensor_tensor(hi, s4[:, :, 0:2], s4[:, :, 2:4], ALU.max))
                link(dve.tensor_tensor(lo, s4[:, :, 0:2], s4[:, :, 2:4], ALU.min))
                gs = r[:, 80:88]
                link(dve.memset(gs, big))
                a4, b4, c4 = r[:, 88:92], gat[:, 0:4], gat[:, 4:8]
                link(dve.tensor_tensor(a4, hi[:, :, 0], hi[:, :, 1], ALU.max))
                link(dve.tensor_tensor(b4, hi[:, :, 0], hi[:, :, 1], ALU.min))
                link(dve.tensor_tensor(c4, lo[:, :, 0], lo[:, :, 1], ALU.max))
                link(dve.tensor_tensor(b4, b4, c4, ALU.max))
                link(dve.tensor_tensor(gs[:, 0:4], a4, b4, ALU.add))
                t8, i8 = r[:, 64:72], r[:, 72:80]
                link(dve.max(t8, gs))
                link(dve.max_index(i8.bitcast(U32), t8, gs))
                link(dve.tensor_copy(a4[:, 0:1], i8[:, 0:1].bitcast(U32)))
                link(dve.tensor_scalar(gat[:, 0:4], slot_no[:, 0:4], a4[:, 0:1], big, ALU.not_equal, ALU.mult))
                for g in range(GROUPS):
                    ins = dve.tensor_scalar(cho[:, 4 * g:4 * g + 4], sel[:, 4 * g:4 * g + 4], gat[:, g:g + 1], None, ALU.add)
                    link(ins)
                link(dve.max(t8, cho))
                link(dve.max_index(i8.bitcast(U32), t8, cho))
                link(dve.tensor_copy(a4[:, 0:2], i8[:, 0:2].bitcast(U32)))
                link(dve.tensor_scalar(gat, slot_no[:, 0:16], a4[:, 0:1], None, ALU.is_equal))
                link(dve.scalar_tensor_tensor(cho, slot_no[:, 0:16], a4[:, 1:2], gat, ALU.is_equal, ALU.add))
                link(dve.tensor_tensor(gat, cho, aff, ALU.mult))
                link(dve.tensor_reduce(a4[:, 2:3], gat, AX.X, ALU.add))
                link(dve.reciprocal(a4[:, 3:4], a4[:, 2:3]))
                dve.tensor_scalar(gat, gat, a4[:, 3:4], None, ALU.mult).then_inc(s_msk, 1)

            dve.wait_ge(s_x, 16)
            for t in range(TT):
                dve.wait_ge(s_wo, t + 1)
                for f in range(2):
                    link(dve.scalar_tensor_tensor(x1[:, t, f * 512:(f + 1) * 512], x_sb[:, t, f * 512:(f + 1) * 512], ALPHA,
                                                  ps[2 * t + f][:, :], ALU.mult, ALU.add))
                if t == 0:
                    dve.wait_ge(s_ln1, 32)
                norm(t, x1[:, t, :], lnv[:, 0, :], lnv[:, 1, :], t + 1).then_inc(s_x1, 1)
                dve.wait_ge(s_x1, t + 1)
                dve.tensor_scalar(acc[:, t, :], x1[:, t, :], ALPHA, None, ALU.mult).then_inc(s_v, 1)
                chain[0] += 1
                route(t)
            dve.wait_ge(s_pos, 1)
            dve.wait_ge(s_msk, TT)
            for t in range(TT):
                link(dve.scalar_tensor_tensor(rt[:, t, 64:80], ps[2][:, 16 * t:16 * t + 16], 1.0, rt[:, t, 32:48], ALU.add,
                                              ALU.mult))
                link(dve.tensor_scalar(rt[:, t, 64:80], rt[:, t, 64:80], -1.0, None, ALU.add))

            def one_hots(p, b):
                src = slot_no[:, SLOTS * b:SLOTS * (b + 1)].unsqueeze(1).to_broadcast([P, 2, SLOTS])
                for t in range(TT):
                    ins = dve.tensor_tensor(hot[:, t, :].rearrange("p (e s) -> p e s", e=2), src,
                                            rt[:, t, bass.ds(p * 2 + 64, 2)].unsqueeze(2).to_broadcast([P, 2, SLOTS]),
                                            ALU.is_equal)
                ins.then_inc(s_hot, 1)

            def gate_hots(p):
                for t in range(TT):
                    ins = dve.tensor_tensor(hotc[:, t, :].rearrange("p (e s) -> p e s", e=2),
                                            hot[:, t, :].rearrange("p (e s) -> p e s", e=2),
                                            rt[:, t, bass.ds(p * 2 + 48, 2)].unsqueeze(2).to_broadcast([P, 2, SLOTS]),
                                            ALU.mult)
                ins.then_inc(s_hotc, 1)

            one_hots(0, 0)
            dve.wait_ge(s_hot, 1)
            gate_hots(0)
            link(dve.tensor_reduce(cnt[:, 0:1], ps[2][:, 32:48], AX.X, ALU.max))
            for b in range(1, ROUNDS):
                link(dve.tensor_scalar(cnt[:, b:b + 1], cnt[:, 0:1], float(SLOTS * b), None, ALU.is_gt))
            dve.tensor_copy(cnt_i[:, :], cnt[:, :]).then_inc(s_cnt, 1)

            def low(n, e, u, place):
                for r in range(BY_VEC):
                    dve.wait_ge(s_hi, n * (SUBS * PER_PAIR) + (SUBS * place + r + 1))
                    dve.tensor_tensor(wlo[:, r, :], ew[e][u][:, r * SUB:(r + 1) * SUB], whi[:, r, :].bitcast(F32),
                                      ALU.subtract).then_inc(s_lo, 1)

            def gathered(n, k, par):
                dve.wait_ge(s_xg, n * 2 + (k + 1))
                for e in range(2):
                    ins = dve.tensor_tensor(xs[:, par, 4 * k:4 * k + 4, e, 1, :],
                                            ps[3 + k][:, :].rearrange("p (a e s) -> p a e s", a=4, e=2)[:, :, e, :],
                                            xs[:, par, 4 * k:4 * k + 4, e, 0, :].bitcast(F32), ALU.subtract)
                ins.then_inc(s_xgl, 1)

            def gate_sum(n, e):
                dve.wait_ge(s_fg, n * 2 + (e + 1))
                dve.tensor_tensor(gsb, ps[0][0:SLOTS, :], gsb, ALU.add).then_inc(s_gs, 1)

            def hidden(n, e):
                dve.wait_ge(s_fu, n * 2 + (e + 1))
                dve.tensor_tensor(usb, ps[1][0:SLOTS, :], usb, ALU.add).then_inc(s_us, 1)
                dve.wait_ge(s_us, n * 2 + (e + 2))
                dve.wait_ge(s_si, n * 2 + (e + 1))
                dve.wait_ge(s_htp, n * 2 + (e + 1))
                dve.tensor_tensor(he, usb, gsb, ALU.mult).then_inc(s_he, 1)

            def hidden_T(n, e):
                dve.wait_ge(s_ht, n * 2 + (e + 1))
                dve.tensor_tensor(heS[:, :, 1, :], ps[2][:, 0:FC * SLOTS].rearrange("p (a b) -> p a b", a=FC),
                                  heS[:, :, 0, :].bitcast(F32), ALU.subtract).then_inc(s_htl, 1)

            def y_sum(n, e):
                for f in range(2):
                    dve.wait_ge(s_ye, n * 4 + (2 * e + f + 1))
                    y = ysb[64 * e:64 * e + 64, f * 512:(f + 1) * 512]
                    dve.tensor_tensor(y, ps[5 + f][64 * e:64 * e + 64, :], y, ALU.add).then_inc(s_ys, 1)

            def accumulate(n):
                dve.wait_ge(s_ac, n * 4 + 1)
                for i, bank in enumerate(SPREAD_BANKS):
                    t, f = i // 2, i % 2
                    dve.wait_ge(s_sp4, n * 4 + (i + 2))
                    a = acc[:, t, f * 512:(f + 1) * 512]
                    dve.tensor_tensor(a, ps[bank][:, :], a, ALU.add).then_inc(s_ac, 1)

            def pair(n, par, pn, bn, first=False, last=False):
                low(n, 0, 1, U0)
                if not first:
                    y_sum(n - 1, 1)
                dve.wait_ge(s_xgp, n * 2 + 2)
                dve.wait_ge(s_hotc, n + 1)
                one_hots(pn, bn)
                low(n, 1, 0, G1)
                hidden(n, 0)
                if not first:
                    accumulate(n - 1)
                gathered(n + 1, 0, 1 - par)
                low(n, 0, 2, D0)
                gate_sum(n, 1)
                hidden_T(n, 0)
                gathered(n + 1, 1, 1 - par)
                low(n, 1, 1, U1)
                y_sum(n, 0)
                if not last:
                    low(n, 0, 0, G0_NEXT)
                hidden(n, 1)
                low(n, 1, 2, D1 - 1 if last else D1)
                if not last:
                    gate_sum(n + 1, 0)
                hidden_T(n, 1)
                dve.wait_ge(s_gp, n + 1)
                dve.tensor_copy(spread, ps[7][:, 0:S].rearrange("p (a b) -> p a b", a=TT)).then_inc(s_g, 1)
                dve.wait_ge(s_hot, n + 2)
                gate_hots(pn)
                if last:
                    y_sum(n, 1)
                    accumulate(n)
                    dve.wait_ge(s_ac, n * 4 + 5)

            def all_pairs(b):
                n = PAIRS * b
                low(n, 0, 0, 0)
                if b == 0:
                    gathered(0, 0, 0)
                    gathered(0, 1, 0)
                gate_sum(n, 0)
                pair(n, 0, 1, b, first=True)
                with dve.Fori(1, PAIRS - 1, 2) as p:
                    pair(p + n, 1, p + 1, b)
                    pair(p + (n + 1), 0, p + 2, b)
                pair(n + PAIRS - 1, 1, 0, b + 1, last=True)

            all_pairs(0)
            dve.wait_ge(s_cnt, 1)
            for b in range(1, ROUNDS):
                with dve.If(dve.value_load(cnt_i[0:1, b:b + 1], min_val=0, max_val=1)):
                    all_pairs(b)
            dve.wait_ge(s_ln2, 32)
            for t in range(TT):
                norm(t, acc[:, t, :], ln2v[:, 0, :], ln2v[:, 1, :], TT + t + 1).then_inc(s_fin, 1)


def laid_out(a):
    a = {k: np.ascontiguousarray(v) for k, v in a.items()}
    x, w_in = a["x"][0], a["w_in"][0]
    sizes = (1024, 1024, HEADS * HD, RANK, IDX_HEADS * IDX_DIM, IDX_DIM, IDX_HEADS, D, D)
    w_xr, w_g, w_q, w_ckv, w_qi, w_ki, w_wi, w_gr, w_ga = np.split(w_in, np.cumsum(sizes)[:-1], axis=1)

    def cols(w, c):
        return w[:, c * P:(c + 1) * P].reshape(KC, P, P).transpose(1, 0, 2).reshape(P, 1024)

    by_kind = {"ckv": w_ckv, "qidx": w_qi, "xr": w_xr, "g": w_g, "gr": w_gr, "ga": w_ga, "q": w_q,
               "pr": a["proj_rnn"][0], "pa": a["proj_att"][0], "kidx": np.concatenate([w_ki, w_ki], axis=1)}
    uk, uv = a["w_uk"][0], a["w_uv"][0]
    pieces = []
    for kind, c in PIECES:
        if kind == "uk":
            w = uk[4 * c:4 * c + 4].reshape(4, CC, P, HD).transpose(2, 0, 1, 3).reshape(P, 1024)
        elif kind == "uv":
            w = uv[:, c * P:(c + 1) * P, :].transpose(1, 0, 2).reshape(P, 1024)
        elif kind == "wo":
            w = a["w_out"][0][c * P:(c + 1) * P, :]
        else:
            w = cols(by_kind[kind], c)
        pieces.append(w)

    def features(v, n=KC):
        return v.reshape(n, P).T

    lru = np.stack([a["lru_wa"][0], a["lru_wx"][0]])
    lru = lru.reshape(2, KC, 2, 64, 64).transpose(2, 0, 3, 1, 4)
    dist = np.maximum(255 - np.arange(3 * P), 0)
    far = BUCKETS // 2 + (np.log(np.maximum(dist, 1).astype(np.float32) / (BUCKETS // 2))
                          / np.log(MAX_DIST / (BUCKETS // 2)) * (BUCKETS // 2)).astype(np.int32)
    bucket = np.where(dist < BUCKETS // 2, dist, np.minimum(far, BUCKETS - 1))
    g = {
        "x": x, "xT": x.T.reshape(KC, P, S).transpose(1, 0, 2), "wp": np.stack(pieces),
        "w_widx": w_wi.reshape(KC, P, IDX_HEADS).transpose(1, 0, 2),
        "conv_w": a["conv_w"][0].reshape(CONV, KC, P).transpose(2, 0, 1), "conv_b": features(a["conv_b"][0]),
        "lru_w": lru, "lru_ba": features(a["lru_ba"][0]), "lru_bx": features(a["lru_bx"][0]),
        "lam": features(a["lru_lambda"][0]), "kvn": features(a["kv_norm"][0], CC),
        "ln1_g": a["ln1_g"][0], "ln1_b": a["ln1_b"][0],
        "w_router": a["w_router"].reshape(KC, P, EXPERTS).transpose(1, 0, 2), "router_bias": a["router_bias"],
        "w_gate": a["exp_w_gate"][0].reshape(EXPERTS, KC, P, FF).transpose(0, 2, 1, 3).reshape(EXPERTS, P, KC * FF),
        "w_up": a["exp_w_up"][0].reshape(EXPERTS, KC, P, FF).transpose(0, 2, 1, 3).reshape(EXPERTS, P, KC * FF),
        "w_down": a["exp_w_down"][0].reshape(EXPERTS, FC, P, D).transpose(0, 2, 1, 3).reshape(EXPERTS, P, FC * D),
        "ln2_g": a["ln2_g"][0], "ln2_b": a["ln2_b"][0], "rel_bias": a["rel_bias"],
        "bucket_hot": (np.arange(BUCKETS)[:, None] == bucket[None]).astype(np.float32),
    }
    return {k: np.ascontiguousarray(v) for k, v in g.items()}


def kernel(**inputs):
    import concourse.bacc as bacc
    from concourse.bass_utils import run_bass_kernel_spmd

    nc = bacc.Bacc("TRN2", target_bir_lowering=False, num_devices=1)
    arrays = laid_out(inputs)
    args = [nc.dram_tensor(n, v.shape, mybir.dt.from_np(v.dtype), kind="ExternalInput").ap() for n, v in arrays.items()]
    args.append(nc.dram_tensor("out", [S, D], F32, kind="ExternalOutput").ap())
    hybrid_layer(nc, *args)
    r = run_bass_kernel_spmd(nc, [arrays], core_ids=[0])
    return r.results[0]["out"].reshape(1, S, D)
```
